# Optimizing a Trainium2 kernel written in Bass

```python
import jax, jax.numpy as jnp
from jax import lax
import numpy as np

D_MODEL = 1024
BATCH = 1
SEQ = 512
DEPTH = 1

HEAD_DIM = 64
A_HEADS = 8
A_KV = 2
WINDOW = 128
BLOCK = 128
B_HEADS = 8
IDX_HEADS = 8
IDX_DIM = 64
TOPK_MAX = 256
D_FF = 2816
D_PLE = 256
EPS = 1e-6
NEG = -1e30

A_Q = A_HEADS * HEAD_DIM
A_KVW = A_KV * HEAD_DIM
B_Q = B_HEADS * HEAD_DIM
B_KVW = HEAD_DIM
I_Q = IDX_HEADS * IDX_DIM
I_K = IDX_DIM
I_W = IDX_HEADS
D_IN = A_Q + 2 * A_KVW + B_Q + 2 * B_KVW + I_Q + I_K + I_W + 2 * D_MODEL

kernel_name = "hybrid_swa_sink_dsa_macaron_ple"

def _split_points():
    sizes = [A_Q, A_KVW, A_KVW, B_Q, B_KVW, B_KVW, I_Q, I_K, I_W, D_MODEL, D_MODEL]
    pts, acc = [], 0
    for s in sizes[:-1]:
        acc += s
        pts.append(acc)
    return pts

def rms_norm(x, g):
    xf = x.astype(jnp.float32)
    y = xf * lax.rsqrt(jnp.mean(xf * xf, axis=-1, keepdims=True) + EPS)
    return (y * g.astype(jnp.float32)).astype(x.dtype)

def swiglu(x, w_in, w_out):
    a, b = jnp.split(x @ w_in, 2, axis=-1)
    return (jax.nn.silu(a) * b) @ w_out

def alibi_slopes():
    n = A_HEADS + B_HEADS
    return 2.0 ** (-8.0 * jnp.arange(1, n + 1, dtype=jnp.float32) / n)

def sliding_window_sink_attention(q, k, v, sink, slopes):
    bsz, t = q.shape[:2]
    nb = t // BLOCK
    r = A_HEADS // A_KV
    qb = q.reshape(bsz, nb, BLOCK, A_KV, r, HEAD_DIM)
    kb = k.reshape(bsz, nb, BLOCK, A_KV, HEAD_DIM)
    vb = v.reshape(bsz, nb, BLOCK, A_KV, HEAD_DIM)
    pad = ((0, 0), (1, 0), (0, 0), (0, 0), (0, 0))
    kc = jnp.concatenate([jnp.pad(kb, pad)[:, :-1], kb], axis=2)
    vc = jnp.concatenate([jnp.pad(vb, pad)[:, :-1], vb], axis=2)
    logits = jnp.einsum('bnqgrd,bnkgd->bngrqk', qb, kc).astype(jnp.float32) * (HEAD_DIM ** -0.5)
    qi = jnp.arange(BLOCK)
    kj = jnp.arange(2 * BLOCK)
    dist = BLOCK + qi[:, None] - kj[None, :]
    s_pos = (jnp.arange(nb)[:, None] - 1) * BLOCK + kj[None, :]
    valid = ((dist >= 0) & (dist < WINDOW))[None] & (s_pos >= 0)[:, None, :]
    sl = slopes.reshape(A_KV, r)[None, None, :, :, None, None]
    logits = logits - sl * dist.astype(jnp.float32)
    logits = jnp.where(valid[None, :, None, None], logits, NEG)
    sink_f = sink.astype(jnp.float32).reshape(A_KV, r)[None, None, :, :, None, None]
    m = jnp.maximum(jnp.max(logits, axis=-1, keepdims=True), sink_f)
    e = jnp.exp(logits - m)
    probs = e / (jnp.sum(e, axis=-1, keepdims=True) + jnp.exp(sink_f - m))
    out = jnp.einsum('bngrqk,bnkgd->bnqgrd', probs.astype(v.dtype), vc)
    return out.reshape(bsz, t, A_HEADS * HEAD_DIM)

def indexed_sparse_attention(q, k, v, qi, ki, wi, slopes):
    bsz, t = q.shape[:2]
    nb = t // BLOCK
    topk = min(TOPK_MAX, t // 4)
    key_pos = jnp.arange(t)
    gather = jax.vmap(lambda tab, idx: tab[idx])

    def to_blocks(a):
        return jnp.moveaxis(a.reshape((bsz, nb, BLOCK) + a.shape[2:]), 1, 0)

    def block(args):
        n, qb, qib, wib = args
        tq = n * BLOCK + jnp.arange(BLOCK)
        rel = jax.nn.relu(jnp.einsum('bqhd,bsd->bqhs', qib, ki).astype(jnp.float32) * (IDX_DIM ** -0.5))
        score = jnp.einsum('bqhs,bqh->bqs', rel, wib.astype(jnp.float32) * (IDX_HEADS ** -0.5))
        causal = key_pos[None, :] <= tq[:, None]
        score = jnp.where(causal[None], score, NEG)
        _, idx = lax.top_k(score, topk)
        kg = gather(k, idx)
        vg = gather(v, idx)
        dist = tq[None, :, None] - idx
        logits = jnp.einsum('bqhd,bqkd->bqhk', qb, kg).astype(jnp.float32) * (HEAD_DIM ** -0.5)
        logits = logits - slopes[None, None, :, None] * dist[:, :, None, :].astype(jnp.float32)
        logits = jnp.where((dist >= 0)[:, :, None, :], logits, NEG)
        probs = jax.nn.softmax(logits, axis=-1)
        return jnp.einsum('bqhk,bqkd->bqhd', probs.astype(v.dtype), vg)

    out = lax.map(block, (jnp.arange(nb), to_blocks(q), to_blocks(qi), to_blocks(wi)))
    return jnp.moveaxis(out, 0, 1).reshape(bsz, t, B_HEADS * HEAD_DIM)

def setup_inputs(seed: int = 0) -> dict:
    key = jax.random.key(seed)
    ks = jax.random.split(key, 20)
    f32 = jnp.float32

    def w(k, shape, fan_in):
        return jax.random.normal(k, shape, f32) * (fan_in ** -0.5)

    def gain(k, shape):
        return 1.0 + 0.05 * jax.random.normal(k, shape, f32)

    return {
        "x": jax.random.normal(ks[0], (BATCH, SEQ, D_MODEL), f32),
        "p": jax.random.normal(ks[1], (DEPTH, BATCH, SEQ, D_PLE), f32),
        "ln_ffn1": gain(ks[2], (DEPTH, D_MODEL)),
        "w_ffn1_in": w(ks[3], (DEPTH, D_MODEL, 2 * D_FF), D_MODEL),
        "w_ffn1_out": w(ks[4], (DEPTH, D_FF, D_MODEL), D_FF),
        "ln_mix": gain(ks[5], (DEPTH, D_MODEL)),
        "w_in": w(ks[6], (DEPTH, D_MODEL, D_IN), D_MODEL),
        "a_sink": 0.5 * jax.random.normal(ks[7], (DEPTH, A_HEADS), f32),
        "w_br_a": w(ks[8], (DEPTH, A_Q, D_MODEL), A_Q),
        "w_br_b": w(ks[9], (DEPTH, B_Q, D_MODEL), B_Q),
        "w_out": w(ks[10], (DEPTH, D_MODEL, D_MODEL), D_MODEL),
        "ln_ffn2": gain(ks[11], (DEPTH, D_MODEL)),
        "w_ffn2_in": w(ks[12], (DEPTH, D_MODEL, 2 * D_FF), D_MODEL),
        "w_ffn2_out": w(ks[13], (DEPTH, D_FF, D_MODEL), D_FF),
        "ln_ple": gain(ks[14], (DEPTH, D_MODEL)),
        "w_ple_gate": w(ks[15], (DEPTH, D_MODEL, D_MODEL), D_MODEL),
        "w_ple_proj": w(ks[16], (DEPTH, D_PLE, D_MODEL), D_PLE),
        "ln_final": gain(ks[17], (D_MODEL,)),
    }

def reference(x, p, ln_ffn1, w_ffn1_in, w_ffn1_out, ln_mix, w_in, a_sink, w_br_a, w_br_b,
              w_out, ln_ffn2, w_ffn2_in, w_ffn2_out, ln_ple, w_ple_gate, w_ple_proj, ln_final):
    bsz, t, _ = x.shape
    slopes = alibi_slopes()
    slopes_a = slopes[:A_HEADS].astype(jnp.float32)
    slopes_b = slopes[A_HEADS:].astype(jnp.float32)
    split_pts = _split_points()
    h = x
    for i in range(DEPTH):
        h = h + 0.5 * swiglu(rms_norm(h, ln_ffn1[i]), w_ffn1_in[i], w_ffn1_out[i])
        u = rms_norm(h, ln_mix[i])
        aq, ak, av, bq, bk, bv, iq, ik, iw, ga, gb = jnp.split(u @ w_in[i], split_pts, axis=-1)
        ya = sliding_window_sink_attention(
            aq.reshape(bsz, t, A_HEADS, HEAD_DIM),
            ak.reshape(bsz, t, A_KV, HEAD_DIM),
            av.reshape(bsz, t, A_KV, HEAD_DIM),
            a_sink[i], slopes_a)
        yb = indexed_sparse_attention(
            bq.reshape(bsz, t, B_HEADS, HEAD_DIM), bk, bv,
            iq.reshape(bsz, t, IDX_HEADS, IDX_DIM), ik, iw, slopes_b)
        mix = jax.nn.sigmoid(ga) * (ya @ w_br_a[i]) + jax.nn.sigmoid(gb) * (yb @ w_br_b[i])
        h = h + mix @ w_out[i]
        h = h + 0.5 * swiglu(rms_norm(h, ln_ffn2[i]), w_ffn2_in[i], w_ffn2_out[i])
        gate = jax.nn.sigmoid(rms_norm(h, ln_ple[i]) @ w_ple_gate[i])
        h = h + gate * (p[i] @ w_ple_proj[i])
    return rms_norm(h, ln_final)


_drawn_inputs = setup_inputs


def setup_inputs(seed=0):
    import zlib

    import numpy as np

    out = dict(_drawn_inputs(seed))
    spreads = {}
    factors = {'a_sink': 8.0, 'ln_ffn2': 3.203, 'ln_ple': 130.806}
    for name, (base, spread) in spreads.items():
        noise = np.random.default_rng([zlib.crc32(name.encode()), seed]).standard_normal(out[name].shape)
        drawn = base * np.exp(spread * noise) if base else spread * noise
        out[name] = __import__('jax').numpy.asarray(drawn.astype(out[name].dtype))
    for name, factor in factors.items():
        out[name] = (out[name] * factor).astype(out[name].dtype)
    return out
```

```python
from contextlib import ExitStack

import numpy as np

import concourse.bass as bass
from concourse import mybir
from concourse.alu_op_type import AluOpType as ALU

ACT = mybir.ActivationFunctionType
F32 = mybir.dt.float32
F32R = mybir.dt.float32r

P = 128
T = 512
NB = T // P
D = 1024
DT = D // P
FF = 2816
FT = FF // P
HD = 64
HEADS = 8
PAIRS = HEADS // 2
TOPK = min(256, T // 4)
PLE_T = 256 // P
EPS = 1e-6
NEG = -1e30
TAKEN = -3.0e38
SLOPES = [float(s) for s in np.float32(2.0) ** (np.float32(-8.0) * np.arange(1, 17, dtype=np.float32) / np.float32(16))]

RAW = 4
SPLIT = 2
K_IN, K_OUT, K_PLE = DT, FT // 2, DT + PLE_T

U_FFN1_IN = 0
U_FFN1_OUT = U_FFN1_IN + 2 * FT
U_PROJ = U_FFN1_OUT + 2 * DT
(IQ, IK, BVIW, BQ, BK, AV, AQ, AK) = (0, 4, 5, 6, 10, 11, 12, 16)
N_PROJ = 17
N_GATES = 2 * DT
U_GATES = U_PROJ + N_PROJ
U_BRANCH = U_GATES + N_GATES
U_MIXOUT = U_BRANCH + DT
U_FFN2_IN = U_MIXOUT + DT
U_FFN2_OUT = U_FFN2_IN + 2 * FT
U_PLE = U_FFN2_OUT + 2 * DT
U_END = U_PLE + DT
N_MID = U_FFN2_IN - U_PROJ
BVW = HD + HEADS

STEPS = [(kind, n, i, g) for kind in "AB" for i in range(PAIRS) for n in range(NB) for g in range(2)]
NS = len(STEPS)
LAG_T, LAG_PV = 2, 3
PER_PAIR = 2 * NB
INDEX = [(n, h) for n in (3, 2, 1) for h in range(HEADS)]
ROUNDS = [(n, k) for n in (3, 2, 1) for k in range(TOPK // 8)]


def unit_rows(u):
    if U_FFN1_OUT <= u < U_PROJ or U_FFN2_OUT <= u < U_PLE:
        return K_OUT
    return K_PLE if u >= U_PLE else K_IN


def layer(nc, x_d, p_d, gains_d, sink_d, w1i_d, w1o_d, wmid_d, w2i_d, w2o_d, wple_d, out_d):
    ctx = ExitStack()
    with ctx:
        def sb(name, shape, dt=F32):
            return ctx.enter_context(nc.sbuf_tensor(name, shape, dt))

        def sem(name):
            return ctx.enter_context(nc.semaphore(name))

        h = sb("h", [P, DT, T])
        x_hi = sb("x_hi", [P, DT, T], F32R)
        x_lo = sb("x_lo", [P, DT, T], F32R)
        raw = sb("raw", [P, RAW, K_OUT * P])
        w_hi = sb("w_hi", [P, SPLIT, K_OUT * P], F32R)
        w_lo = sb("w_lo", [P, SPLIT, K_OUT * P], F32R)
        R = sb("R", [P, T])
        squares = sb("squares", [P, 2, T])
        sumsq = sb("sumsq", [P, T])
        rstd_wide = sb("rstd_wide", [P, NB, P])
        std = sb("std", [P, NB])
        rstd = sb("rstd", [P, NB])
        gains = sb("gains", [P, 5, DT])
        sink = sb("sink", [P, HEADS])
        ones = sb("ones", [P, 1])
        eps = sb("eps", [P, 1])
        ident = sb("ident", [P, P])
        row_max = sb("row_max", [P, 4])
        neg_max = sb("neg_max", [P, 4])
        row_sum = sb("row_sum", [P, 4])
        sink_exp = sb("sink_exp", [P, 4])
        row_rcp = sb("row_rcp", [P, 4])
        top8 = sb("top8", [P, 8])

        base = nc.sbuf_base
        base = (base + 31) // 32 * 32
        region = nc.sbuf_usable_end - base

        class Place:

            def __init__(self, at=0):
                self.at = at

            def __call__(self, name, shape, dt=F32):
                t = nc.alloc_sbuf_tensor_at(name, shape, dt, offset=base + self.at)
                self.at += 4 * int(np.prod(shape[1:]))
                self.at = (self.at + 31) // 32 * 32
                assert self.at <= region, (name, self.at, region)
                return t

        ffn = Place()
        g_hi = ffn("g_hi", [P, FT, T], F32R)
        g_lo = ffn("g_lo", [P, FT, T], F32R)
        ffn_work = ffn.at
        a_val = ffn("a_val", [P, 2, T])
        a_sig = ffn("a_sig", [P, 2, T])
        ab = ffn("ab", [P, 2, T])
        mid = Place()
        gates = mid("gates", [P, N_GATES, T])
        q_place = mid.at
        qA = mid("qA", [P, PAIRS, T])
        qB = mid("qB", [P, PAIRS, T])
        qI = mid("qI", [P, PAIRS, T])
        biasA = mid("biasA", [P, HEADS, 2 * P])
        over_q = Place(q_place)
        yA_hi = over_q("yA_hi", [P, PAIRS, T], F32R)
        yB_hi = over_q("yB_hi", [P, PAIRS, T], F32R)
        yB_lo = over_q("yB_lo", [P, PAIRS, T], F32R)
        yA_lo = over_q("yA_lo", [P, PAIRS, T], F32R)
        temps = mid.at
        kA = mid("kA", [P, T])
        kB = mid("kB", [P, T])
        kI = mid("kI", [P, T])
        vA = mid("vA", [P, NB, P])
        vB = mid("vB", [P, NB, HD])
        w_idx = mid("w_idx", [P, NB, HEADS])
        score_at = [None, 0, 2 * P, 5 * P]
        score = mid("score", [P, 9 * P])
        taken = mid("taken", [P, T])
        dist = mid("dist", [P, T])
        causal = mid("causal", [P, T])
        window = mid("window", [P, 2 * P])
        probs = mid("probs", [P, 4, T])
        biasB = mid("biasB", [P, 2, T])
        probsT = mid("probsT", [P, 2, T])
        merge = Place(temps)
        mix_hi = merge("mix_hi", [P, DT, T], F32R)
        mix_lo = merge("mix_lo", [P, DT, T], F32R)
        br = merge("br", [P, 2, T])
        ple_p = Place(ffn_work)
        p_raw = ple_p("p_raw", [P, PLE_T, T])
        p_hi = ple_p("p_hi", [P, PLE_T, T], F32R)
        p_lo = ple_p("p_lo", [P, PLE_T, T], F32R)
        ple = Place()
        pg_val = ple("pg_val", [P, 2, T])
        pg_sig = ple("pg_sig", [P, 2, T])
        result = ple("result", [P, DT, T])

        acc = ctx.enter_context(nc.psum_tensor("acc", [P, 4, T], F32))
        att = ctx.enter_context(nc.psum_tensor("att", [P, 4, T], F32))
        stat_bank, r_bank = att[:, 3, 0:NB], att[:, 2, :]
        y_bank, pt_bank = att[:, 3, :], att[:, 2, :]

        raw_in = [sem(f"raw_in{s}") for s in range(RAW)]
        x_in = [sem(f"x_in{m}") for m in range(DT)]
        gains_in, sink_in, p_in = sem("gains_in"), sem("sink_in"), sem("p_in")
        out_done = sem("out_done")
        consts_done = sem("consts_done")
        hi_done = sem("hi_done")
        lo_done = sem("lo_done")
        unit_done = sem("unit_done")
        x_hi_done, x_lo_done = sem("x_hi_done"), sem("x_lo_done")
        sq_done, sumsq_done = sem("sq_done"), sem("sumsq_done")
        stat_done, std_done, rstd_done = sem("stat_done"), sem("std_done"), sem("rstd_done")
        wide_done, r_full, r_done = sem("wide_done"), sem("r_full"), sem("r_done")
        h_done = sem("h_done")
        a_done, sig_done, b_done = sem("a_done"), sem("sig_done"), sem("b_done")
        ab_done, g_done = sem("ab_done"), sem("g_done")
        g_hi_done, g_lo_done = sem("g_hi_done"), sem("g_lo_done")
        proj_done = sem("proj_done")
        w_idx_done = sem("w_idx_done")
        masks_done = sem("masks_done")
        biasA_done = sem("biasA_done")
        idx_full, relu_done, idx_added = sem("idx_full"), sem("relu_done"), sem("idx_added")
        top8_done, took8 = sem("top8_done"), sem("took8")
        untaken_done, mask_done = sem("untaken_done"), sem("mask_done")
        s_full, biasB_done, logits_done = sem("s_full"), sem("biasB_done"), sem("logits_done")
        neg_max_done, exp_done, sink_exp_done = sem("neg_max_done"), sem("exp_done"), sem("sink_exp_done")
        sum_done, rcp_done, probs_done = sem("sum_done"), sem("rcp_done"), sem("probs_done")
        pt_full, pt_copied, pv_done = sem("pt_full"), sem("pt_copied"), sem("pv_done")
        y_hi_done, y_lo_done = sem("y_hi_done"), sem("y_lo_done")
        gate_sig = sem("gate_sig")
        br_a, br_b, mix_done = sem("br_a"), sem("br_b"), sem("mix_done")
        mix_hi_done, mix_lo_done = sem("mix_hi_done"), sem("mix_lo_done")
        p_hi_done, p_lo_done = sem("p_hi_done"), sem("p_lo_done")
        pg_val_done, pg_sig_done, pg_mul = sem("pg_val_done"), sem("pg_sig_done"), sem("pg_mul")
        result_done = sem("result_done")

        block = ctx.enter_context(nc.Block())

        def keys_of(kind, n):
            first = max(n - 1, 0) if kind == "A" else 0
            return first, n + 1 - first

        def tile(t, j):
            return t[:, j, :] if isinstance(j, int) else t[:, bass.ds(j, 1), :].rearrange("p a c -> p (a c)")

        @block.sync
        def _(sp):
            def load(w_d, i, c, first, rows):
                s = c % RAW
                if not (isinstance(i, int) and c + 4 * i < RAW):
                    sp.wait_ge(lo_done, 4 * i + (c - RAW + 1))
                n = 4 * i + (c - first)
                src = w_d[n] if isinstance(n, int) else w_d[bass.ds(n, 1), :, :].rearrange("u p c -> (u p) c")
                sp.dma_start(raw[:, s, 0:rows * P], src).then_inc(raw_in[s], 16)

            def loads(w_d, first, n, rows):
                peel = 4 if first == 0 else 0
                for c in range(first, first + peel):
                    load(w_d, 0, c, first, rows)
                with sp.Fori(peel // 4, n // 4) as i:
                    for r in range(4):
                        load(w_d, i, first + r, first, rows)
                for c in range(first + n // 4 * 4, first + n):
                    load(w_d, 0, c, first, rows)

            loads(w1i_d, U_FFN1_IN, 2 * FT, K_IN)
            loads(w1o_d, U_FFN1_OUT, 2 * DT, K_OUT)
            loads(wmid_d, U_PROJ, N_MID, K_IN)
            loads(w2i_d, U_FFN2_IN, 2 * FT, K_IN)
            loads(w2o_d, U_FFN2_OUT, 2 * DT, K_OUT)
            sp.wait_ge(g_lo_done, 2 * FT)
            sp.dma_start(p_raw[:], p_d).then_inc(p_in, 16)
            loads(wple_d, U_PLE, DT, K_PLE)
            for m in range(DT):
                sp.wait_ge(result_done, m + 1)
                sp.dma_start(out_d[m], result[:, m, :]).then_inc(out_done, 16)
            sp.wait_ge(out_done, 16 * DT)

        @block.gpsimd
        def _(pool):
            nc.gpsimd.memset(ident[:], 0.0).then_inc(consts_done, 1)
            nc.gpsimd.memset(ones[:], 1.0).then_inc(consts_done, 1)
            nc.gpsimd.memset(eps[:], EPS).then_inc(consts_done, 1)
            pool.wait_ge(consts_done, 3)
            nc.gpsimd.affine_select(out=ident[:], in_=ident[:], compare_op=ALU.not_equal, fill=1.0, base=0,
                                    pattern=[[-1, P]], channel_multiplier=1).then_inc(consts_done, 1)

            def lo(i, c, rows):
                w = slice(0, rows * P)
                pool.wait_ge(hi_done, 4 * i + (c + 1))
                nc.gpsimd.tensor_tensor(w_lo[:, c % SPLIT, w], raw[:, c % RAW, w],
                                        w_hi[:, c % SPLIT, w].bitcast(F32), ALU.subtract).then_inc(lo_done, 1)

            def los(first, n, rows):
                with pool.Fori(0, n // 4) as i:
                    for r in range(4):
                        lo(i, first + r, rows)
                for c in range(first + n // 4 * 4, first + n):
                    lo(0, c, rows)

            los(U_FFN1_IN, 2 * FT, K_IN)
            los(U_FFN1_OUT, 2 * DT, K_OUT)
            los(U_PROJ, 4, K_IN)
            nc.gpsimd.iota(dist[:], pattern=[[-1, T]], base=T - P, channel_multiplier=1,
                           allow_small_or_imprecise_dtypes=True).then_inc(masks_done, 1)
            nc.gpsimd.memset(causal[:], 0.0).then_inc(masks_done, 1)
            nc.gpsimd.memset(window[:], 0.0).then_inc(masks_done, 1)
            los(U_PROJ + 4, 4, K_IN)
            pool.wait_ge(masks_done, 3)
            nc.gpsimd.affine_select(out=causal[:], in_=causal[:], compare_op=ALU.is_ge, fill=NEG, base=T - P,
                                    pattern=[[-1, T]], channel_multiplier=1).then_inc(masks_done, 1)
            nc.gpsimd.affine_select(out=window[:], in_=window[:], compare_op=ALU.is_ge, fill=NEG, base=P,
                                    pattern=[[-1, 2 * P]], channel_multiplier=1).then_inc(masks_done, 1)
            pool.wait_ge(masks_done, 5)
            nc.gpsimd.affine_select(out=window[:], in_=window[:], compare_op=ALU.is_ge, fill=NEG, base=-1,
                                    pattern=[[1, 2 * P]], channel_multiplier=-1).then_inc(masks_done, 1)
            los(U_PROJ + 8, N_MID - 8, K_IN)
            los(U_FFN2_IN, 2 * FT, K_IN)
            los(U_FFN2_OUT, 2 * DT, K_OUT)
            los(U_PLE, DT, K_PLE)

        @block.scalar
        def _(act):
            def hi(i, c):
                if isinstance(i, int) and c + 4 * i >= U_END:
                    return
                w = slice(0, unit_rows(c) * P)
                act.wait_ge(raw_in[c % RAW], 16 * i + 16 * (c // RAW + 1))
                if not (isinstance(i, int) and c + 4 * i < SPLIT):
                    act.wait_ge(unit_done, 4 * i + (c - SPLIT + 1))
                nc.scalar.activation(w_hi[:, c % SPLIT, w], raw[:, c % RAW, w], ACT.Copy).then_inc(hi_done, 1)

            def squared(k, m):
                out = sumsq[:, :] if m == 0 else squares[:, m % 2, :]
                if m >= 3:
                    act.wait_ge(sumsq_done, 7 * k + m - 2)
                nc.scalar.activation(out, h[:, m, :], ACT.Square).then_inc(sq_done, 1)

            def prepare(k, m):
                nc.scalar.activation(x_hi[:, m, :], h[:, m, :], ACT.Copy,
                                     scale=gains[:, k, m:m + 1]).then_inc(x_hi_done, 1)
                squared(k, m)

            def root(k):
                act.wait_ge(stat_done, k + 1)
                nc.scalar.activation(std[:], stat_bank, ACT.Sqrt, bias=eps[:, 0:1],
                                     scale=1.0 / D).then_inc(std_done, 1)

            def take_r(k):
                act.wait_ge(r_full, k + 1)
                nc.scalar.activation(R[:], r_bank, ACT.Copy).then_inc(r_done, 1)

            def ffn_in(u0, t0, k):
                def sig(i, r):
                    t = t0 + r
                    act.wait_ge(a_done, 2 * i + (t + 1))
                    nc.scalar.activation(a_sig[:, t % 2, :], a_val[:, t % 2, :], ACT.Sigmoid).then_inc(sig_done, 1)

                def gated(i, r):
                    t = t0 + r
                    act.wait_ge(g_done, 2 * i + (t + 1))
                    j = 2 * i + r
                    nc.scalar.activation(tile(g_hi, j), ab[:, t % 2, :], ACT.Copy).then_inc(g_hi_done, 1)

                root(k)
                hi(0, u0 + 2)
                hi(0, u0 + 3)
                take_r(k)
                sig(0, 0)
                gated(0, 0)
                hi(0, u0 + 4)
                sig(0, 1)
                hi(0, u0 + 5)
                gated(0, 1)
                with act.Fori(1, FT // 2 - 1) as i:
                    for r in range(2):
                        hi(i, u0 + 2 * r + 2)
                        sig(i, r)
                        hi(i, u0 + 2 * r + 3)
                        gated(i, r)
                for r in range(2):
                    c = u0 + 2 * FT - 4 + 2 * r
                    hi(0, c + 2)
                    sig(FT // 2 - 1, r)
                    hi(0, c + 3)
                    gated(FT // 2 - 1, r)

            def ffn_out(u0, h0, k):
                for m in range(DT):
                    hi(0, u0 + 2 * m + 2)
                    hi(0, u0 + 2 * m + 3)
                    act.wait_ge(h_done, h0 + m + 1)
                    prepare(k, m)

            for m in range(DT):
                act.dma_start(h[:, m, :], x_d[:, m, :]).then_inc(x_in[m], 16)
                if m == 0:
                    act.dma_start(gains[:], gains_d).then_inc(gains_in, 16)
            act.dma_start(sink[:], sink_d).then_inc(sink_in, 16)
            hi(0, 0)
            act.wait_ge(gains_in, 16)
            for m in range(DT):
                act.wait_ge(x_in[m], 16)
                prepare(0, m)
                if m == 3:
                    hi(0, 1)
            act.wait_ge(consts_done, 4)
            ffn_in(U_FFN1_IN, 0, 0)
            ffn_out(U_FFN1_OUT, 0, 1)

            u0 = U_PROJ
            root(1)
            hi(0, u0 + 2)
            hi(0, u0 + 3)
            take_r(1)

            def relu(t):
                n, _ = INDEX[t]
                w = slice(0, (n + 1) * P)
                act.wait_ge(idx_full, t + 1)
                if t >= 2:
                    act.wait_ge(idx_added, t - 1)
                nc.scalar.activation(probs[:, t % 2, w], att[:, t % 4, w], ACT.Relu).then_inc(relu_done, 1)

            after = {BVIW: range(0, 8), BQ: range(8, 16), BQ + 1: range(16, 24)}
            for u in range(2, N_PROJ):
                hi(0, u0 + u + 2)
                for t in after.get(u, ()):
                    relu(t)

            def exps(s):
                kind, n, i, g = STEPS[s]
                w = slice(0, keys_of(kind, n)[1] * P)
                head = i + 4 * g
                act.wait_ge(neg_max_done, s + 1)
                nc.scalar.activation(probs[:, s % 4, w], probs[:, s % 4, w], ACT.Exp, bias=neg_max[:, s % 4:s % 4 + 1],
                                     accum_out=row_sum[:, s % 4:s % 4 + 1]).then_inc(exp_done, 1)
                if kind == "A":
                    nc.scalar.activation(sink_exp[:, s % 4:s % 4 + 1], neg_max[:, s % 4:s % 4 + 1], ACT.Exp,
                                         bias=sink[:, head:head + 1]).then_inc(sink_exp_done, 1)

            def copy_pt(s):
                kind, n, i, g = STEPS[s]
                w = slice(0, keys_of(kind, n)[1] * P)
                act.wait_ge(pt_full, s + 1)
                if s >= 2:
                    act.wait_ge(pv_done, s - 1)
                nc.scalar.activation(probsT[:, s % 2, w], pt_bank[:, w], ACT.Copy).then_inc(pt_copied, 1)

            def y_hi(pair):
                act.wait_ge(pv_done, PER_PAIR * (pair + 1))
                dst = (yA_hi if pair < PAIRS else yB_hi)[:, pair % PAIRS, :]
                nc.scalar.activation(dst, y_bank, ACT.Copy).then_inc(y_hi_done, 1)

            act.wait_ge(sink_in, 16)
            for s in range(NS + LAG_PV):
                if s < NS:
                    exps(s)
                if 0 <= s - LAG_T < NS:
                    copy_pt(s - LAG_T)
                if s >= LAG_PV and (s - LAG_PV) % PER_PAIR == PER_PAIR - 1:
                    y_hi((s - LAG_PV) // PER_PAIR)
                if s < NS and s % 4 == 3:
                    hi(0, U_GATES + s // 4 + 2)

            def sigmoids(m):
                for gt in (m, DT + m):
                    if m == 0:
                        act.wait_ge(proj_done, N_PROJ + N_GATES)
                    nc.scalar.activation(gates[:, gt, :], gates[:, gt, :], ACT.Sigmoid).then_inc(gate_sig, 1)

            sigmoids(0)
            for m in range(DT):
                hi(0, U_BRANCH + m + 2)
                act.wait_ge(mix_done, m + 1)
                nc.scalar.activation(mix_hi[:, m, :], br[:, 0, :], ACT.Copy).then_inc(mix_hi_done, 1)
                if m + 1 < DT:
                    sigmoids(m + 1)
            for m in range(DT):
                hi(0, U_MIXOUT + m + 2)
                act.wait_ge(h_done, DT + m + 1)
                prepare(2, m)
            ffn_in(U_FFN2_IN, FT, 2)
            ffn_out(U_FFN2_OUT, 2 * DT, 3)

            act.wait_ge(p_in, 16)
            for j in range(PLE_T):
                nc.scalar.activation(p_hi[:, j, :], p_raw[:, j, :], ACT.Copy).then_inc(p_hi_done, 1)
            root(3)
            hi(0, U_PLE + 2)
            hi(0, U_PLE + 3)
            take_r(3)
            for m in range(DT):
                if m >= 2:
                    hi(0, U_PLE + m + 2)
                act.wait_ge(pg_val_done, m + 1)
                nc.scalar.activation(pg_sig[:, m % 2, :], pg_val[:, m % 2, :], ACT.Sigmoid).then_inc(pg_sig_done, 1)
                act.wait_ge(h_done, 3 * DT + m + 1)
                squared(4, m)
            root(4)

        @block.vector
        def _(dve):
            def add_squares(k, m):
                if m == 0:
                    return
                dve.wait_ge(sq_done, DT * k + m + 1)
                if m >= 2:
                    dve.wait_ge(sumsq_done, 7 * k + m - 1)
                nc.vector.tensor_tensor(sumsq[:], sumsq[:], squares[:, m % 2, :], ALU.add).then_inc(sumsq_done, 1)

            def prepare(k, m):
                dve.wait_ge(x_hi_done, DT * k + m + 1)
                nc.vector.scalar_tensor_tensor(x_lo[:, m, :], h[:, m, :], gains[:, k, m:m + 1],
                                               x_hi[:, m, :].bitcast(F32), ALU.mult, ALU.subtract).then_inc(x_lo_done, 1)
                add_squares(k, m)

            def norm(k):
                dve.wait_ge(std_done, k + 1)
                nc.vector.reciprocal(rstd[:], std[:]).then_inc(rstd_done, 1)
                dve.wait_ge(rstd_done, k + 1)
                nc.vector.tensor_copy(rstd_wide[:], rstd[:].unsqueeze(2).broadcast_to([P, NB, P])).then_inc(wide_done, 1)
                dve.wait_ge(r_done, k + 1)

            def ffn_in(u0, t0, k):
                def a_part(i, c, r):
                    t = t0 + r
                    dve.wait_ge(unit_done, 4 * i + (c + 1))
                    nc.vector.tensor_tensor(a_val[:, t % 2, :], acc[:, (2 * r) % 4, :], R[:], ALU.mult).then_inc(a_done, 1)

                def b_part(i, c, r):
                    t = t0 + r
                    now = 2 * i + (t + 1)
                    dve.wait_ge(unit_done, 4 * i + (c + 1))
                    nc.vector.tensor_tensor(ab[:, t % 2, :], acc[:, (2 * r + 1) % 4, :], R[:], ALU.mult).then_inc(b_done, 1)
                    dve.wait_ge(b_done, now)
                    nc.vector.tensor_tensor(ab[:, t % 2, :], ab[:, t % 2, :], a_val[:, t % 2, :], ALU.mult).then_inc(ab_done, 1)
                    dve.wait_ge(ab_done, now)
                    dve.wait_ge(sig_done, now)
                    nc.vector.tensor_tensor(ab[:, t % 2, :], ab[:, t % 2, :], a_sig[:, t % 2, :], ALU.mult).then_inc(g_done, 1)
                    dve.wait_ge(g_hi_done, now)
                    j = 2 * i + r
                    nc.vector.tensor_tensor(tile(g_lo, j), ab[:, t % 2, :], tile(g_hi, j).bitcast(F32),
                                            ALU.subtract).then_inc(g_lo_done, 1)

                norm(k)
                with dve.Fori(0, FT // 2) as i:
                    for r in range(2):
                        a_part(i, u0 + 2 * r, r)
                        b_part(i, u0 + 2 * r + 1, r)

            def ffn_out(u0, h0, k):
                for m in range(DT):
                    dve.wait_ge(unit_done, u0 + 2 * m + 2)
                    nc.vector.scalar_tensor_tensor(h[:, m, :], acc[:, m % 2, :], 0.5, h[:, m, :],
                                                   ALU.mult, ALU.add).then_inc(h_done, 1)
                    prepare(k, m)

            for m in range(DT):
                prepare(0, m)
            ffn_in(U_FFN1_IN, 0, 0)
            ffn_out(U_FFN1_OUT, 0, 1)
            norm(1)

            def bank(a):
                return acc[:, (a + 2) % 4, :]

            def query(dst, u, a):
                dve.wait_ge(unit_done, U_PROJ + u + 1)
                nc.vector.scalar_tensor_tensor(dst, bank(a), HD ** -0.5, R[:], ALU.mult, ALU.mult).then_inc(proj_done, 1)

            def scaled(dst, u, a):
                dve.wait_ge(unit_done, U_PROJ + u + 1)
                nc.vector.tensor_tensor(dst, bank(a), R[:], ALU.mult).then_inc(proj_done, 1)

            def values(dst, u, a, width, at):
                dve.wait_ge(unit_done, U_PROJ + u + 1)
                src = bank(a)[:, 0:NB * width].rearrange("p (n c) -> p n c", n=NB)
                if width == BVW:
                    nc.vector.scalar_tensor_tensor(w_idx[:], src[:, :, HD:BVW], HEADS ** -0.5,
                                                   rstd[:].unsqueeze(2).broadcast_to([P, NB, HEADS]),
                                                   ALU.mult, ALU.mult).then_inc(w_idx_done, 1)
                nc.vector.tensor_tensor(dst, src[:, :, 0:at], rstd[:].unsqueeze(2).broadcast_to([P, NB, at]),
                                        ALU.mult).then_inc(proj_done, 1)

            def add_index(t):
                n, hh = INDEX[t]
                width = (n + 1) * P
                out = score[:, score_at[n]:score_at[n] + width]
                if t == 0:
                    dve.wait_ge(w_idx_done, 1)
                    dve.wait_ge(masks_done, 6)
                dve.wait_ge(relu_done, t + 1)
                if hh:
                    dve.wait_ge(idx_added, t)
                nc.vector.scalar_tensor_tensor(out, probs[:, t % 2, 0:width], w_idx[:, n, hh:hh + 1],
                                               out if hh else causal[:, T - width:T], ALU.mult, ALU.add).then_inc(idx_added, 1)

            rounds = list(enumerate(ROUNDS))

            def select(count):
                for r, (n, k) in [rounds.pop(0) for _ in range(min(count, len(rounds)))]:
                    width = (n + 1) * P
                    sc = score[:, score_at[n]:score_at[n] + width]
                    left = taken[:, 0:width]
                    src = left if k else sc
                    if k:
                        dve.wait_ge(took8, r)
                    elif r:
                        dve.wait_ge(mask_done, 3 - n)
                    else:
                        dve.wait_ge(idx_added, len(INDEX))
                    nc.vector.max(top8[:], src).then_inc(top8_done, 1)
                    dve.wait_ge(top8_done, r + 1)
                    nc.vector.match_replace(left, top8[:], src, TAKEN).then_inc(took8, 1)
                    if k == TOPK // 8 - 1:
                        dve.wait_ge(took8, r + 1)
                        nc.vector.tensor_tensor(sc, left, sc, ALU.is_equal).then_inc(untaken_done, 1)
                        dve.wait_ge(untaken_done, 4 - n)
                        nc.vector.tensor_scalar(sc, sc, NEG, None, ALU.mult).then_inc(mask_done, 1)

            order = ([(query, qI[:, i, :], IQ + i) for i in range(PAIRS)] + [(scaled, kI[:], IK), (values, vB[:], BVIW)]
                     + [(query, qB[:, i, :], BQ + i) for i in range(PAIRS)] + [(scaled, kB[:], BK), (values, vA[:], AV)]
                     + [(query, qA[:, i, :], AQ + i) for i in range(PAIRS)] + [(scaled, kA[:], AK)])
            for a, (what, dst, u) in enumerate(order):
                if what is values:
                    values(dst, u, a, BVW if u == BVIW else P, HD if u == BVIW else P)
                else:
                    what(dst, u, a)
                if BVIW <= u < BVIW + 3:
                    for t in range(8 * (u - BVIW), 8 * (u - BVIW) + 8):
                        add_index(t)
                elif u == BQ + 2:
                    for hh in range(HEADS):
                        nc.vector.scalar_tensor_tensor(biasA[:, 2 * (hh % 4) + hh // 4, :], dist[:, 2 * P:T], -SLOPES[hh], window[:],
                                                       ALU.mult, ALU.add).then_inc(biasA_done, 1)
                elif u > BQ + 2:
                    select(3)

            def logits(s):
                kind, n, i, g = STEPS[s]
                head = i + 4 * g
                width = keys_of(kind, n)[1] * P
                w = slice(0, width)
                c = slice(s % 4, s % 4 + 1)
                if kind == "A":
                    bias = biasA[:, 2 * i + g, 2 * P - width:2 * P]
                else:
                    b = s - NS // 2
                    mask = score[:, score_at[n]:score_at[n] + width] if n else causal[:, T - P:T]
                    bias = biasB[:, s % 2, w]
                    if b >= 2:
                        dve.wait_ge(logits_done, s - 1)
                    nc.vector.scalar_tensor_tensor(bias, dist[:, T - width:T], -SLOPES[HEADS + head], mask,
                                                   ALU.mult, ALU.add).then_inc(biasB_done, 1)
                    dve.wait_ge(biasB_done, b + 1)
                dve.wait_ge(s_full, s + 1)
                if s >= 4:
                    dve.wait_ge(pt_full, s - 3)
                if s == 0:
                    dve.wait_ge(biasA_done, HEADS)
                nc.vector.tensor_tensor_reduce(out=probs[:, s % 4, w], in0=att[:, s % 2, w], in1=bias, scale=1.0,
                                               scalar=-3.4e38, op0=ALU.add, op1=ALU.max,
                                               accum_out=row_max[:, c]).then_inc(logits_done, 1)
                dve.wait_ge(logits_done, s + 1)
                if kind == "A":
                    nc.vector.tensor_scalar(neg_max[:, c], row_max[:, c], sink[:, head:head + 1], -1.0,
                                            ALU.max, ALU.mult).then_inc(neg_max_done, 1)
                else:
                    nc.vector.tensor_scalar(neg_max[:, c], row_max[:, c], -1.0, None, ALU.mult).then_inc(neg_max_done, 1)

            def normalise(s):
                kind, n, i, g = STEPS[s]
                w = slice(0, keys_of(kind, n)[1] * P)
                c = slice(s % 4, s % 4 + 1)
                dve.wait_ge(exp_done, s + 1)
                if kind == "A":
                    dve.wait_ge(sink_exp_done, s + 1)
                    nc.vector.tensor_tensor(row_sum[:, c], row_sum[:, c], sink_exp[:, c], ALU.add).then_inc(sum_done, 1)
                    dve.wait_ge(sum_done, s + 1)
                nc.vector.reciprocal(row_rcp[:, c], row_sum[:, c]).then_inc(rcp_done, 1)
                dve.wait_ge(rcp_done, s + 1)
                nc.vector.tensor_scalar(probs[:, s % 4, w], probs[:, s % 4, w], row_rcp[:, c], None,
                                        ALU.mult).then_inc(probs_done, 1)

            def y_lo(pair):
                dst, hi_ = (yA_lo, yA_hi) if pair < PAIRS else (yB_lo, yB_hi)
                i = pair % PAIRS
                dve.wait_ge(y_hi_done, pair + 1)
                nc.vector.tensor_tensor(dst[:, i, :], y_bank, hi_[:, i, :].bitcast(F32), ALU.subtract).then_inc(y_lo_done, 1)

            dve.wait_ge(sink_in, 16)
            for s in range(NS + LAG_PV):
                if s < NS:
                    logits(s)
                if 1 <= s <= NS:
                    normalise(s - 1)
                if s < NS // 2:
                    select(1)
                if s == NS // 2 - 1:
                    select(len(rounds))
                if s >= LAG_PV and (s - LAG_PV) % PER_PAIR == PER_PAIR - 1:
                    y_lo((s - LAG_PV) // PER_PAIR)
                if s % 4 == 0 and 0 < s <= NS:
                    gt = s // 4 - 1
                    scaled(gates[:, gt, :], N_PROJ + gt, N_PROJ + gt)

            for m in range(DT):
                pair = 2 * (m % 2)
                dve.wait_ge(unit_done, U_BRANCH + m + 1)
                dve.wait_ge(gate_sig, 2 * m + 2)
                if m:
                    dve.wait_ge(mix_lo_done, m)
                nc.vector.tensor_tensor(br[:, 0, :], acc[:, pair, :], gates[:, m, :], ALU.mult).then_inc(br_a, 1)
                nc.vector.tensor_tensor(br[:, 1, :], acc[:, pair + 1, :], gates[:, DT + m, :], ALU.mult).then_inc(br_b, 1)
                dve.wait_ge(br_b, m + 1)
                nc.vector.tensor_tensor(br[:, 0, :], br[:, 0, :], br[:, 1, :], ALU.add).then_inc(mix_done, 1)
                dve.wait_ge(mix_hi_done, m + 1)
                nc.vector.tensor_tensor(mix_lo[:, m, :], br[:, 0, :], mix_hi[:, m, :].bitcast(F32),
                                        ALU.subtract).then_inc(mix_lo_done, 1)
            for m in range(DT):
                dve.wait_ge(unit_done, U_MIXOUT + m + 1)
                nc.vector.tensor_tensor(h[:, m, :], acc[:, m % 4, :], h[:, m, :], ALU.add).then_inc(h_done, 1)
                prepare(2, m)
            ffn_in(U_FFN2_IN, FT, 2)
            ffn_out(U_FFN2_OUT, 2 * DT, 3)

            for j in range(PLE_T):
                dve.wait_ge(p_hi_done, j + 1)
                nc.vector.tensor_tensor(p_lo[:, j, :], p_raw[:, j, :], p_hi[:, j, :].bitcast(F32),
                                        ALU.subtract).then_inc(p_lo_done, 1)
            norm(3)
            for m in range(DT):
                b = (2 * m + 2) % 4
                dve.wait_ge(unit_done, U_PLE + m + 1)
                nc.vector.tensor_tensor(pg_val[:, m % 2, :], acc[:, b, :], R[:], ALU.mult).then_inc(pg_val_done, 1)
                dve.wait_ge(pg_sig_done, m + 1)
                nc.vector.tensor_tensor(pg_val[:, m % 2, :], acc[:, b + 1, :], pg_sig[:, m % 2, :],
                                        ALU.mult).then_inc(pg_mul, 1)
                dve.wait_ge(pg_mul, m + 1)
                nc.vector.tensor_tensor(h[:, m, :], h[:, m, :], pg_val[:, m % 2, :], ALU.add).then_inc(h_done, 1)
                add_squares(4, m)

            dve.wait_ge(std_done, 5)
            nc.vector.reciprocal(rstd[:], std[:]).then_inc(rstd_done, 1)
            dve.wait_ge(rstd_done, 5)
            nc.vector.tensor_copy(rstd_wide[:], rstd[:].unsqueeze(2).broadcast_to([P, NB, P])).then_inc(wide_done, 1)
            dve.wait_ge(r_full, 5)
            for m in range(DT):
                nc.vector.scalar_tensor_tensor(result[:, m, :], h[:, m, :], gains[:, 4, m:m + 1], r_bank,
                                               ALU.mult, ALU.mult).then_inc(result_done, 1)

        @block.tensor
        def _(pe):
            mm = nc.tensor.matmul

            def wait_unit(i, c):
                pe.wait_ge(lo_done, 4 * i + (c + 1))

            def product(out, c, b, m_hi, m_lo, start, stop):
                w = slice(b * P, b * P + P)
                mm(out, w_hi[:, c % SPLIT, w], m_hi, start=start, stop=False)
                mm(out, w_hi[:, c % SPLIT, w], m_lo, start=False, stop=False)
                return mm(out, w_lo[:, c % SPLIT, w], m_hi, start=False, stop=stop)

            def x_unit(i, c, out, x0=None):
                wait_unit(i, c)
                for b in range(DT):
                    if x0 is not None:
                        pe.wait_ge(x_lo_done, x0 + b + 1)
                    last = product(out, c, b, x_hi[:, b, :], x_lo[:, b, :], b == 0, b == DT - 1)
                last.then_inc(unit_done, 1)

            def stats(k):
                pe.wait_ge(sumsq_done, 7 * (k + 1))
                for n in range(NB):
                    last = mm(stat_bank[:, n:n + 1], sumsq[:, n * P:(n + 1) * P], ones[:, 0:1], start=True, stop=True)
                last.then_inc(stat_done, 1)

            def spread(k):
                pe.wait_ge(wide_done, k + 1)
                for n in range(NB):
                    last = mm(r_bank[:, n * P:(n + 1) * P], rstd_wide[:, n, :], ident[:], start=True, stop=True)
                last.then_inc(r_full, 1)

            def ffn_in(u0, t0, k):
                for r in range(4):
                    if t0 and r == 0:
                        pe.wait_ge(h_done, 2 * DT - 2)
                    if t0 and r == 2:
                        pe.wait_ge(h_done, 2 * DT)
                    x_unit(0, u0 + r, acc[:, r, :], DT * k if r == 0 else None)
                    if r == 0:
                        stats(k)
                    if r == 1:
                        spread(k)
                with pe.Fori(1, FT // 2) as i:
                    for r in range(4):
                        if r % 2 == 0:
                            pe.wait_ge(b_done, 2 * i + (t0 + r // 2 - 1))
                        x_unit(i, u0 + r, acc[:, r, :])

            def ffn_out(u0, t0, h0):
                for m in range(DT):
                    out = acc[:, m % 2, :]
                    if m < 2:
                        pe.wait_ge(b_done, t0 + FT - 1)
                    else:
                        pe.wait_ge(h_done, h0 + m - 1)
                    for half in range(2):
                        c = u0 + 2 * m + half
                        wait_unit(0, c)
                        for b in range(K_OUT):
                            j = half * K_OUT + b
                            if m == 0:
                                pe.wait_ge(g_lo_done, t0 + j + 1)
                            last = product(out, c, b, g_hi[:, j, :], g_lo[:, j, :], j == 0, j == FT - 1)
                        last.then_inc(unit_done, 1)

            pe.wait_ge(consts_done, 4)
            ffn_in(U_FFN1_IN, 0, 0)
            ffn_out(U_FFN1_OUT, 0, 0)

            def bank(a):
                return acc[:, (a + 2) % 4, :]

            def bank_free(a):
                if a in (2, 3):
                    pe.wait_ge(h_done, DT - 3 + a)
                elif a >= 4:
                    pe.wait_ge(proj_done, a - 3)

            def token_major(c, out, width):
                wait_unit(0, c)
                for n in range(NB):
                    t = slice(n * P, (n + 1) * P)
                    o = out[:, n * width:(n + 1) * width]
                    for b in range(DT):
                        w = slice(b * P, b * P + width)
                        mm(o, x_hi[:, b, t], w_hi[:, c % SPLIT, w], start=(b == 0), stop=False)
                        mm(o, x_hi[:, b, t], w_lo[:, c % SPLIT, w], start=False, stop=False)
                        last = mm(o, x_lo[:, b, t], w_hi[:, c % SPLIT, w], start=False, stop=(b == DT - 1))
                last.then_inc(unit_done, 1)

            def index_products(n):
                for hh in range(HEADS):
                    t = INDEX.index((n, hh))
                    half = slice(HD * (hh // 4), HD * (hh // 4) + HD)
                    if t == 0:
                        pe.wait_ge(proj_done, IK + 1)
                    if t >= 4:
                        pe.wait_ge(relu_done, t - 3)
                    mm(att[:, t % 4, 0:(n + 1) * P], qI[half, hh % 4, n * P:(n + 1) * P], kI[half, 0:(n + 1) * P],
                       start=True, stop=True).then_inc(idx_full, 1)

            for u in range(N_PROJ):
                bank_free(u)
                if u == AV:
                    token_major(U_PROJ + u, bank(u), P)
                elif u == BVIW:
                    token_major(U_PROJ + u, bank(u), BVW)
                else:
                    x_unit(0, U_PROJ + u, bank(u), DT if u == 0 else None)
                if u == 0:
                    stats(1)
                if u == 1:
                    spread(1)
                if u == BVIW:
                    index_products(3)
                if u == BQ:
                    index_products(2)
                if u == BQ + 1:
                    index_products(1)

            def scores(s):
                kind, n, i, g = STEPS[s]
                first, count = keys_of(kind, n)
                half = slice(HD * g, HD * g + HD)
                q, k_ = (qA, kA) if kind == "A" else (qB, kB)
                if s == 0:
                    pe.wait_ge(proj_done, N_PROJ)
                    pe.wait_ge(relu_done, len(INDEX))
                if s >= 2:
                    pe.wait_ge(logits_done, s - 1)
                mm(att[:, s % 2, 0:count * P], q[half, i, n * P:(n + 1) * P], k_[half, first * P:(first + count) * P],
                   start=True, stop=True).then_inc(s_full, 1)

            def transposes(s):
                kind, n, i, g = STEPS[s]
                pe.wait_ge(probs_done, s + 1)
                if s >= 1:
                    pe.wait_ge(pt_copied, s)
                for b in range(keys_of(kind, n)[1]):
                    w = slice(b * P, (b + 1) * P)
                    last = nc.tensor.transpose(pt_bank[:, w], probs[:, s % 4, w], ident[:])
                last.then_inc(pt_full, 1)

            def weighted(s):
                kind, n, i, g = STEPS[s]
                first, count = keys_of(kind, n)
                half = slice(HD * g, HD * g + HD)
                pe.wait_ge(pt_copied, s + 1)
                if s % PER_PAIR == 0 and s:
                    pe.wait_ge(y_lo_done, s // PER_PAIR)
                for b in range(count):
                    v = vA[:, first + b, half] if kind == "A" else vB[:, first + b, :]
                    last = mm(y_bank[half, n * P:(n + 1) * P], v, probsT[:, s % 2, b * P:(b + 1) * P],
                              start=(b == 0), stop=(b == count - 1))
                last.then_inc(pv_done, 1)

            for s in range(NS + LAG_PV):
                if s < NS:
                    scores(s)
                if s >= LAG_PV:
                    weighted(s - LAG_PV)
                if LAG_T <= s < NS + LAG_T:
                    transposes(s - LAG_T)
                if s < NS:
                    gt, quarter = divmod(s, 4)
                    c = U_GATES + gt
                    if quarter == 0:
                        bank_free(N_PROJ + gt)
                        wait_unit(0, c)
                    for b in (2 * quarter, 2 * quarter + 1):
                        last = product(bank(N_PROJ + gt), c, b, x_hi[:, b, :], x_lo[:, b, :], b == 0, b == DT - 1)
                    if quarter == 3:
                        last.then_inc(unit_done, 1)

            for m in range(DT):
                pair = 2 * (m % 2)
                c = U_BRANCH + m
                if m < 2:
                    pe.wait_ge(proj_done, N_PROJ + N_GATES - 1 + m)
                else:
                    pe.wait_ge(br_b, m - 1)
                wait_unit(0, c)
                for b in range(2 * PAIRS):
                    y_h, y_l = (yA_hi, yA_lo) if b < PAIRS else (yB_hi, yB_lo)
                    i = b % PAIRS
                    if m == 0:
                        pe.wait_ge(y_lo_done, b + 1)
                    last = product(acc[:, pair + b // PAIRS, :], c, b, y_h[:, i, :], y_l[:, i, :],
                                   i == 0, i == PAIRS - 1)
                last.then_inc(unit_done, 1)
            for m in range(DT):
                c = U_MIXOUT + m
                if m < 4:
                    pe.wait_ge(br_b, DT - 1 + m // 2)
                else:
                    pe.wait_ge(h_done, DT + m - 3)
                wait_unit(0, c)
                for b in range(DT):
                    if m == 0:
                        pe.wait_ge(mix_lo_done, b + 1)
                    last = product(acc[:, m % 4, :], c, b, mix_hi[:, b, :], mix_lo[:, b, :], b == 0, b == DT - 1)
                last.then_inc(unit_done, 1)

            ffn_in(U_FFN2_IN, FT, 2)
            ffn_out(U_FFN2_OUT, FT, 2 * DT)

            for m in range(DT):
                b0 = (2 * m + 2) % 4
                c = U_PLE + m
                if m == 1:
                    pe.wait_ge(h_done, 3 * DT)
                if m >= 2:
                    pe.wait_ge(pg_mul, m - 1)
                wait_unit(0, c)
                for b in range(DT):
                    if m == 0:
                        pe.wait_ge(x_lo_done, 3 * DT + b + 1)
                    product(acc[:, b0, :], c, b, x_hi[:, b, :], x_lo[:, b, :], b == 0, b == DT - 1)
                if m == 0:
                    pe.wait_ge(p_lo_done, PLE_T)
                for j in range(PLE_T):
                    last = product(acc[:, b0 + 1, :], c, DT + j, p_hi[:, j, :], p_lo[:, j, :], j == 0, j == PLE_T - 1)
                last.then_inc(unit_done, 1)
                if m == 0:
                    stats(3)
                if m == 1:
                    spread(3)
            stats(4)
            spread(4)


def _columns(w, cols, width=P):
    k = w.shape[0] // P
    out = np.zeros((len(cols), P, k, P), w.dtype)
    for n, c in enumerate(cols):
        out[n, :, :, 0:len(c)] = w[:, c].reshape(k, P, len(c)).transpose(1, 0, 2)
    return out.reshape(len(cols), P, k * P)


def kernel(**inputs):
    import concourse.bacc as bacc
    from concourse.bass_utils import run_bass_kernel_spmd

    a = {n: np.asarray(v) for n, v in inputs.items()}
    tiles = [np.arange(m * P, (m + 1) * P) for m in range(DT)]

    def feature_major(x):
        return np.ascontiguousarray(x.T.reshape(-1, P, T).transpose(1, 0, 2))

    def ffn_in(w):
        return _columns(w, [np.arange(s * FF + j * P, s * FF + (j + 1) * P) for j in range(FT) for s in range(2)])

    def ffn_out(w):
        u = _columns(w, tiles).reshape(DT, P, 2, K_OUT * P)
        return np.ascontiguousarray(u.transpose(0, 2, 1, 3)).reshape(2 * DT, P, K_OUT * P)

    sizes = dict(aq=512, ak=128, av=128, bq=512, bk=64, bv=64, iq=512, ik=64, iw=8, ga=D, gb=D)
    at, n = {}, 0
    for name, size in sizes.items():
        at[name] = n + np.arange(size)
        n += size
    pair = [np.concatenate([np.arange(i * HD, (i + 1) * HD), np.arange((i + 4) * HD, (i + 5) * HD)])
            for i in range(PAIRS)]
    proj = ([at["iq"][c] for c in pair] + [np.concatenate([at["ik"], at["ik"]]), np.concatenate([at["bv"], at["iw"]])]
            + [at["bq"][c] for c in pair] + [np.concatenate([at["bk"], at["bk"]]), at["av"]]
            + [at["aq"][c] for c in pair] + [at["ak"]])
    gate = [at[s][c] for s in ("ga", "gb") for c in tiles]
    rows = np.concatenate(pair)
    branches = np.concatenate([_columns(a["w_br_a"][0][rows], tiles), _columns(a["w_br_b"][0][rows], tiles)], axis=2)
    mid = np.concatenate([_columns(a["w_in"][0], proj + gate), branches, _columns(a["w_out"][0], tiles)])
    ple = np.concatenate([_columns(a["w_ple_gate"][0], tiles), _columns(a["w_ple_proj"][0], tiles)], axis=2)
    gains = np.stack([a["ln_ffn1"][0], a["ln_mix"][0], a["ln_ffn2"][0], a["ln_ple"][0], a["ln_final"]])

    arrays = {
        "x": feature_major(a["x"][0]),
        "p": feature_major(a["p"][0, 0]),
        "gains": np.ascontiguousarray(gains.reshape(5, DT, P).transpose(2, 0, 1)),
        "sink": np.ascontiguousarray(np.broadcast_to(a["a_sink"][0], (P, HEADS))),
        "w_ffn1_in": ffn_in(a["w_ffn1_in"][0]),
        "w_ffn1_out": ffn_out(a["w_ffn1_out"][0]),
        "w_mid": mid,
        "w_ffn2_in": ffn_in(a["w_ffn2_in"][0]),
        "w_ffn2_out": ffn_out(a["w_ffn2_out"][0]),
        "w_ple": ple,
    }
    nc = bacc.Bacc("TRN2", target_bir_lowering=False, num_devices=1)
    args = [nc.dram_tensor(f"in_{n}", v.shape, mybir.dt.from_np(v.dtype), kind="ExternalInput").ap()
            for n, v in arrays.items()]
    args.append(nc.dram_tensor("out_t", (DT, P, T), F32, kind="ExternalOutput").ap())
    layer(nc, *args)
    r = run_bass_kernel_spmd(nc, [{f"in_{n}": v for n, v in arrays.items()}], core_ids=[0])
    out = r.results[0]["out_t"]
    return np.ascontiguousarray(out.reshape(D, T).T).reshape(1, T, D)
```

```python
from contextlib import ExitStack

import numpy as np

import concourse.bass as bass
from concourse import mybir
from concourse.alu_op_type import AluOpType as ALU

ACT = mybir.ActivationFunctionType
F32 = mybir.dt.float32
F32R = mybir.dt.float32r

P = 128
T = 512
NB = T // P
D = 1024
DT = D // P
FF = 2816
FT = FF // P
HD = 64
HEADS = 8
PAIRS = HEADS // 2
TOPK = min(256, T // 4)
PLE_T = 256 // P
EPS = 1e-6
NEG = -1e30
TAKEN = -3.0e38
SLOPES = [float(s) for s in np.float32(2.0) ** (np.float32(-8.0) * np.arange(1, 17, dtype=np.float32) / np.float32(16))]

RAW = 4
SPLIT = 2
K_IN, K_OUT, K_PLE = DT, FT // 2, DT + PLE_T

U_FFN1_IN = 0
U_FFN1_OUT = U_FFN1_IN + 2 * FT
U_PROJ = U_FFN1_OUT + 2 * DT
(IBK, BVIW, IQ, BQ, AV, AQ, AK) = (0, 1, 2, 6, 10, 11, 15)
N_PROJ = 16
N_GATES = 2 * DT
U_GATES = U_PROJ + N_PROJ
U_BRANCH = U_GATES + N_GATES
U_MIXOUT = U_BRANCH + DT
U_FFN2_IN = U_MIXOUT + DT
U_FFN2_OUT = U_FFN2_IN + 2 * FT
U_PLE = U_FFN2_OUT + 2 * DT
U_END = U_PLE + DT
N_MID = U_FFN2_IN - U_PROJ
BVW = HD + HEADS

STEPS = [(kind, n, i, g) for kind in "AB" for i in range(PAIRS) for n in range(NB) for g in range(2)]
NS = len(STEPS)
LAG_T, LAG_PV = 3, 4
PER_PAIR = 2 * NB
INDEX = [(n, h) for n in (3, 2, 1) for h in range(HEADS)]
ROUNDS = [(n, k) for n in (3, 2, 1) for k in range(TOPK // 8)]


def unit_rows(u):
    if U_FFN1_OUT <= u < U_PROJ or U_FFN2_OUT <= u < U_PLE:
        return K_OUT
    return K_PLE if u >= U_PLE else K_IN


def layer(nc, x_d, p_d, gains_d, sink_d, w1i_d, w1o_d, wmid_d, w2i_d, w2o_d, wple_d, out_d):
    ctx = ExitStack()
    with ctx:
        def sb(name, shape, dt=F32):
            return ctx.enter_context(nc.sbuf_tensor(name, shape, dt))

        def sem(name):
            return ctx.enter_context(nc.semaphore(name))

        h = sb("h", [P, DT, T])
        x_hi = sb("x_hi", [P, DT, T], F32R)
        x_lo = sb("x_lo", [P, DT, T], F32R)
        raw = sb("raw", [P, RAW, K_OUT * P])
        w_hi = sb("w_hi", [P, SPLIT, K_OUT * P], F32R)
        w_lo = sb("w_lo", [P, SPLIT, K_OUT * P], F32R)
        R = sb("R", [P, T])
        squares = sb("squares", [P, 2, T])
        sumsq = sb("sumsq", [P, T])
        rstd_wide = sb("rstd_wide", [P, NB, P])
        std = sb("std", [P, NB])
        rstd = sb("rstd", [P, NB])
        gains = sb("gains", [P, 5, DT])
        sink = sb("sink", [P, HEADS])
        ones = sb("ones", [P, 1])
        eps = sb("eps", [P, 1])
        ident = sb("ident", [P, P])
        row_max = sb("row_max", [P, 4])
        neg_max = sb("neg_max", [P, 4])
        row_sum = sb("row_sum", [P, 4])
        sink_exp = sb("sink_exp", [P, 4])
        row_rcp = sb("row_rcp", [P, 4])
        top8 = sb("top8", [P, 8])
        unused = sb("unused", [P, 1])

        base = nc.sbuf_base
        base = (base + 31) // 32 * 32
        region = nc.sbuf_usable_end - base

        class Place:

            def __init__(self, at=0):
                self.at = at

            def __call__(self, name, shape, dt=F32):
                t = nc.alloc_sbuf_tensor_at(name, shape, dt, offset=base + self.at)
                self.at += 4 * int(np.prod(shape[1:]))
                self.at = (self.at + 31) // 32 * 32
                assert self.at <= region, (name, self.at, region)
                return t

        ffn = Place()
        g_hi = ffn("g_hi", [P, FT, T], F32R)
        g_lo = ffn("g_lo", [P, FT, T], F32R)
        ffn_work = ffn.at
        a_val = ffn("a_val", [P, 2, T])
        a_sig = ffn("a_sig", [P, 2, T])
        ab = ffn("ab", [P, 2, T])
        mid = Place()
        gates = mid("gates", [P, N_GATES, T])
        q_place = mid.at
        qA = mid("qA", [P, PAIRS, T])
        qB = mid("qB", [P, PAIRS, T])
        qI = mid("qI", [P, PAIRS, T])
        biasA = mid("biasA", [P, HEADS, 2 * P])
        over_q = Place(q_place)
        yA_hi = over_q("yA_hi", [P, PAIRS, T], F32R)
        yB_hi = over_q("yB_hi", [P, PAIRS, T], F32R)
        yB_lo = over_q("yB_lo", [P, PAIRS, T], F32R)
        yA_lo = over_q("yA_lo", [P, PAIRS, T], F32R)
        temps = mid.at
        kA = mid("kA", [P, T])
        kB = mid("kB", [P, T])
        kI = mid("kI", [P, T])
        vA = mid("vA", [P, NB, P])
        vB = mid("vB", [P, NB, HD])
        w_idx = mid("w_idx", [P, NB, HEADS])
        score_at = [None, 0, 2 * P, 5 * P]
        score = mid("score", [P, 9 * P])
        taken = mid("taken", [P, T])
        dist = mid("dist", [P, T])
        causal = mid("causal", [P, T])
        window = mid("window", [P, 2 * P])
        probs = mid("probs", [P, 4, T])
        biasB = mid("biasB", [P, 2, T])
        probsT = mid("probsT", [P, 2, T])
        bvT, avT = probs[:, 2, :], probs[:, 3, :]
        merge = Place(temps)
        mix_hi = merge("mix_hi", [P, DT, T], F32R)
        mix_lo = merge("mix_lo", [P, DT, T], F32R)
        br = merge("br", [P, 2, T])
        ple_p = Place(ffn_work)
        p_raw = ple_p("p_raw", [P, PLE_T, T])
        p_hi = ple_p("p_hi", [P, PLE_T, T], F32R)
        p_lo = ple_p("p_lo", [P, PLE_T, T], F32R)
        ple = Place()
        pg_val = ple("pg_val", [P, 2, T])
        pg_sig = ple("pg_sig", [P, 2, T])
        result = ple("result", [P, DT, T])

        acc = ctx.enter_context(nc.psum_tensor("acc", [P, 4, T], F32))
        att = ctx.enter_context(nc.psum_tensor("att", [P, 4, T], F32))
        stat_bank, r_bank = att[:, 3, 0:NB], att[:, 2, :]
        y_bank, pt_bank = att[:, 3, :], att[:, 2, :]

        raw_in = [sem(f"raw_in{s}") for s in range(RAW)]
        x_in = [sem(f"x_in{m}") for m in range(DT)]
        gains_in, sink_in, p_in = sem("gains_in"), sem("sink_in"), sem("p_in")
        out_done = sem("out_done")
        consts_done = sem("consts_done")
        hi_done = sem("hi_done")
        lo_done = sem("lo_done")
        unit_done = sem("unit_done")
        x_hi_done, x_lo_done = sem("x_hi_done"), sem("x_lo_done")
        sq_done, sumsq_done = sem("sq_done"), sem("sumsq_done")
        stat_done, std_done, rstd_done = sem("stat_done"), sem("std_done"), sem("rstd_done")
        wide_done, r_full, r_done = sem("wide_done"), sem("r_full"), sem("r_done")
        h_done = sem("h_done")
        a_done, sig_done, b_done = sem("a_done"), sem("sig_done"), sem("b_done")
        ab_done, g_done = sem("ab_done"), sem("g_done")
        g_hi_done, g_lo_done = sem("g_hi_done"), sem("g_lo_done")
        proj_done = sem("proj_done")
        k_copied = sem("k_copied")
        v_full = sem("v_full")
        v_done, w_idx_done = sem("v_done"), sem("w_idx_done")
        masks_done = sem("masks_done")
        biasA_done = sem("biasA_done")
        idx_full, relu_done, idx_added = sem("idx_full"), sem("relu_done"), sem("idx_added")
        top8_done, took8 = sem("top8_done"), sem("took8")
        untaken_done, mask_done = sem("untaken_done"), sem("mask_done")
        s_full, biasB_done, logits_done = sem("s_full"), sem("biasB_done"), sem("logits_done")
        neg_max_done, exp_done, sink_exp_done = sem("neg_max_done"), sem("exp_done"), sem("sink_exp_done")
        sum_done, rcp_done, probs_done = sem("sum_done"), sem("rcp_done"), sem("probs_done")
        pt_full, pt_copied, pv_done = sem("pt_full"), sem("pt_copied"), sem("pv_done")
        y_hi_done, y_lo_done = sem("y_hi_done"), sem("y_lo_done")
        gate_sig = sem("gate_sig")
        br_a, br_b, mix_done = sem("br_a"), sem("br_b"), sem("mix_done")
        mix_hi_done, mix_lo_done = sem("mix_hi_done"), sem("mix_lo_done")
        p_hi_done, p_lo_done = sem("p_hi_done"), sem("p_lo_done")
        pg_full = sem("pg_full")
        pg_val_done, pg_sig_done, pg_mul = sem("pg_val_done"), sem("pg_sig_done"), sem("pg_mul")
        result_done = sem("result_done")

        block = ctx.enter_context(nc.Block())

        def keys_of(kind, n):
            first = max(n - 1, 0) if kind == "A" else 0
            return first, n + 1 - first

        def tile(t, j):
            return t[:, j, :] if isinstance(j, int) else t[:, bass.ds(j, 1), :].rearrange("p a c -> p (a c)")

        def gain(k, m):
            return gains[:, k, m:m + 1] if isinstance(m, int) else gains[:, k, bass.ds(m, 1)]

        def groups(eng, first_unit, n, body):
            last = n // 4 - 1
            body(0, first_unit)
            with eng.Fori(1, last) as i:
                body(i, first_unit)
            body(0, first_unit + 4 * last)

        @block.sync
        def _(sp):
            def load(w_d, i, c, first, rows):
                s = c % RAW
                if not (isinstance(i, int) and c + 4 * i < RAW):
                    sp.wait_ge(lo_done, 4 * i + (c - RAW + 1))
                n = 4 * i + (c - first)
                src = w_d[n] if isinstance(n, int) else w_d[bass.ds(n, 1), :, :].rearrange("u p c -> (u p) c")
                sp.dma_start(raw[:, s, 0:rows * P], src).then_inc(raw_in[s], 16)

            def loads(w_d, first, n, rows):
                with sp.Fori(1 if first == 0 else 0, n // 4) as i:
                    for r in range(4):
                        load(w_d, i, first + r, first, rows)

            def load_x(m):
                sp.dma_start(h[:, m, :], x_d[:, m, :]).then_inc(x_in[m], 16)

            load(w1i_d, 0, 0, 0, K_IN)
            for m in range(4):
                load_x(m)
            load(w1i_d, 0, 1, 0, K_IN)
            for m in range(4, DT):
                load_x(m)
            load(w1i_d, 0, 2, 0, K_IN)
            load(w1i_d, 0, 3, 0, K_IN)
            loads(w1i_d, U_FFN1_IN, 2 * FT, K_IN)
            loads(w1o_d, U_FFN1_OUT, 2 * DT, K_OUT)
            loads(wmid_d, U_PROJ, N_MID, K_IN)
            loads(w2i_d, U_FFN2_IN, 2 * FT, K_IN)
            loads(w2o_d, U_FFN2_OUT, 2 * DT, K_OUT)
            sp.wait_ge(g_lo_done, 2 * FT)
            sp.dma_start(p_raw[:], p_d).then_inc(p_in, 16)
            loads(wple_d, U_PLE, DT, K_PLE)
            for m in range(DT):
                sp.wait_ge(result_done, m + 1)
                sp.dma_start(out_d[m], result[:, m, :]).then_inc(out_done, 16)
            sp.wait_ge(out_done, 16 * DT)

        @block.gpsimd
        def _(pool):
            nc.gpsimd.memset(ident[:], 0.0).then_inc(consts_done, 1)
            nc.gpsimd.memset(ones[:], 1.0).then_inc(consts_done, 1)
            nc.gpsimd.memset(eps[:], EPS).then_inc(consts_done, 1)
            pool.wait_ge(consts_done, 3)
            nc.gpsimd.affine_select(out=ident[:], in_=ident[:], compare_op=ALU.not_equal, fill=1.0, base=0,
                                    pattern=[[-1, P]], channel_multiplier=1).then_inc(consts_done, 1)

            def lo(i, c, rows):
                w = slice(0, rows * P)
                pool.wait_ge(hi_done, 4 * i + (c + 1))
                nc.gpsimd.tensor_tensor(w_lo[:, c % SPLIT, w], raw[:, c % RAW, w],
                                        w_hi[:, c % SPLIT, w].bitcast(F32), ALU.subtract).then_inc(lo_done, 1)

            def los(first, n, rows, start=0):
                with pool.Fori(start, n // 4) as i:
                    for r in range(4):
                        lo(i, first + r, rows)

            pool.wait_ge(lo_done, 1)
            for c in range(1, 4):
                lo(0, c, K_IN)
            los(U_FFN1_IN, 2 * FT, K_IN, start=1)
            los(U_FFN1_OUT, 2 * DT, K_OUT)
            los(U_PROJ, 4, K_IN)
            nc.gpsimd.iota(dist[:], pattern=[[-1, T]], base=T - P, channel_multiplier=1,
                           allow_small_or_imprecise_dtypes=True).then_inc(masks_done, 1)
            nc.gpsimd.memset(causal[:], 0.0).then_inc(masks_done, 1)
            nc.gpsimd.memset(window[:], 0.0).then_inc(masks_done, 1)
            los(U_PROJ + 4, 4, K_IN)
            pool.wait_ge(masks_done, 3)
            nc.gpsimd.affine_select(out=causal[:], in_=causal[:], compare_op=ALU.is_ge, fill=NEG, base=T - P,
                                    pattern=[[-1, T]], channel_multiplier=1).then_inc(masks_done, 1)
            nc.gpsimd.affine_select(out=window[:], in_=window[:], compare_op=ALU.is_ge, fill=NEG, base=P,
                                    pattern=[[-1, 2 * P]], channel_multiplier=1).then_inc(masks_done, 1)
            pool.wait_ge(masks_done, 5)
            nc.gpsimd.affine_select(out=window[:], in_=window[:], compare_op=ALU.is_ge, fill=NEG, base=-1,
                                    pattern=[[1, 2 * P]], channel_multiplier=-1).then_inc(masks_done, 1)
            los(U_PROJ + 8, N_MID - 8, K_IN)
            los(U_FFN2_IN, 2 * FT, K_IN)
            los(U_FFN2_OUT, 2 * DT, K_OUT)
            los(U_PLE, DT, K_PLE)

        @block.scalar
        def _(act):
            def hi(i, c):
                if isinstance(i, int) and c + 4 * i >= U_END:
                    return
                w = slice(0, unit_rows(c) * P)
                act.wait_ge(raw_in[c % RAW], 16 * i + 16 * (c // RAW + 1))
                if not (isinstance(i, int) and c + 4 * i < SPLIT):
                    act.wait_ge(unit_done, 4 * i + (c - SPLIT + 1))
                nc.scalar.activation(w_hi[:, c % SPLIT, w], raw[:, c % RAW, w], ACT.Copy).then_inc(hi_done, 1)

            def squares_free(k, m):
                if not (isinstance(m, int) and m < 3):
                    act.wait_ge(sumsq_done, m + (7 * k - 2))

            def squared(k, m, slot=None, waits=True):
                slot = m % 2 if slot is None else slot
                first = isinstance(m, int) and m == 0
                if waits:
                    squares_free(k, m)
                nc.scalar.activation(sumsq[:] if first else squares[:, slot, :], tile(h, m),
                                     ACT.Square).then_inc(sq_done, 1)

            def x_part(k, m):
                nc.scalar.activation(tile(x_hi, m), tile(h, m), ACT.Copy,
                                     scale=gain(k, m)).then_inc(x_hi_done, 1)

            def prepare(k, m):
                x_part(k, m)
                squared(k, m)

            def root(k):
                act.wait_ge(stat_done, k + 1)
                nc.scalar.activation(std[:], stat_bank, ACT.Sqrt, bias=eps[:, 0:1],
                                     scale=1.0 / D).then_inc(std_done, 1)

            def take_r(k):
                act.wait_ge(r_full, k + 1)
                nc.scalar.activation(R[:], r_bank, ACT.Copy).then_inc(r_done, 1)

            def ffn_in(u0, t0, k):
                def sig(i, r):
                    t = t0 + r
                    act.wait_ge(a_done, 2 * i + (t + 1))
                    nc.scalar.activation(a_sig[:, t % 2, :], a_val[:, t % 2, :], ACT.Sigmoid).then_inc(sig_done, 1)

                def gated(i, r):
                    t = t0 + r
                    act.wait_ge(g_done, 2 * i + (t + 1))
                    j = 2 * i + r
                    nc.scalar.activation(tile(g_hi, j), ab[:, t % 2, :], ACT.Copy).then_inc(g_hi_done, 1)

                if k:
                    root(k)
                hi(0, u0 + 2)
                if k:
                    take_r(k)
                else:
                    root(k)
                hi(0, u0 + 3)
                if not k:
                    take_r(k)
                sig(0, 0)
                gated(0, 0)
                hi(0, u0 + 4)
                sig(0, 1)
                hi(0, u0 + 5)
                gated(0, 1)
                with act.Fori(1, FT // 2 - 1) as i:
                    for r in range(2):
                        hi(i, u0 + 2 * r + 2)
                        sig(i, r)
                        hi(i, u0 + 2 * r + 3)
                        gated(i, r)
                for r in range(2):
                    c = u0 + 2 * FT - 4 + 2 * r
                    hi(0, c + 2)
                    sig(FT // 2 - 1, r)
                    hi(0, c + 3)
                    gated(FT // 2 - 1, r)

            def ffn_out(u0, h0, k):
                def pair_of_tiles(i, c):
                    for r in range(2):
                        m = 2 * i + (c - u0) // 2 + r
                        hi(i, c + 2 * r + 2)
                        hi(i, c + 2 * r + 3)
                        squares_free(k, m)
                        act.wait_ge(h_done, m + (h0 + 1))
                        x_part(k, m)
                        squared(k, m, r, waits=False)

                groups(act, u0, 2 * DT, pair_of_tiles)

            act.dma_start(gains[:], gains_d).then_inc(gains_in, 16)
            act.dma_start(sink[:], sink_d).then_inc(sink_in, 16)
            act.wait_ge(consts_done, 4)
            nc.scalar.activation(unused[:], ones[:], ACT.Sqrt)
            hi(0, 0)
            act.wait_ge(gains_in, 16)
            for m in range(DT):
                act.wait_ge(x_in[m], 16)
                x_part(0, m)
                if m == 2:
                    hi(0, 1)
            for m in range(DT):
                squared(0, m)
            ffn_in(U_FFN1_IN, 0, 0)
            ffn_out(U_FFN1_OUT, 0, 1)

            u0 = U_PROJ
            root(1)
            hi(0, u0 + 2)
            take_r(1)
            hi(0, u0 + 3)

            def relu(t):
                n, _ = INDEX[t]
                w = slice(0, (n + 1) * P)
                act.wait_ge(idx_full, t + 1)
                if t >= 2:
                    act.wait_ge(idx_added, t - 1)
                nc.scalar.activation(probs[:, t % 2, w], att[:, t % 4, w], ACT.Relu).then_inc(relu_done, 1)

            for u in range(2, N_PROJ):
                if BQ <= u < BQ + 3:
                    for t in range(HEADS * (u - BQ), HEADS * (u - BQ + 1)):
                        relu(t)
                hi(0, u0 + u + 2)
                if u == 2:
                    act.wait_ge(proj_done, 2)
                    act.dma_start(kI[HD:P, :], kI[0:HD, :]).then_inc(k_copied, 16)
                    act.dma_start(kB[0:HD, :], kB[HD:P, :]).then_inc(k_copied, 16)
                if u == BQ + 3:
                    nc.scalar.activation(unused[:], ones[:], ACT.Exp)

            def exps(s):
                kind, n, i, g = STEPS[s]
                w = slice(0, keys_of(kind, n)[1] * P)
                head = i + 4 * g
                act.wait_ge(neg_max_done, s + 1)
                nc.scalar.activation(probs[:, s % 4, w], probs[:, s % 4, w], ACT.Exp, bias=neg_max[:, s % 4:s % 4 + 1],
                                     accum_out=row_sum[:, s % 4:s % 4 + 1]).then_inc(exp_done, 1)
                if kind == "A":
                    nc.scalar.activation(sink_exp[:, s % 4:s % 4 + 1], neg_max[:, s % 4:s % 4 + 1], ACT.Exp,
                                         bias=sink[:, head:head + 1]).then_inc(sink_exp_done, 1)

            def normalise(s):
                kind, n, i, g = STEPS[s]
                w = slice(0, keys_of(kind, n)[1] * P)
                act.wait_ge(rcp_done, s + 1)
                nc.scalar.activation(probs[:, s % 4, w], probs[:, s % 4, w], ACT.Copy,
                                     scale=row_rcp[:, s % 4:s % 4 + 1]).then_inc(probs_done, 1)

            def copy_pt(s):
                kind, n, i, g = STEPS[s]
                w = slice(0, keys_of(kind, n)[1] * P)
                act.wait_ge(pt_full, s + 1)
                if s >= 2:
                    act.wait_ge(pv_done, s - 1)
                nc.scalar.activation(probsT[:, s % 2, w], pt_bank[:, w], ACT.Copy).then_inc(pt_copied, 1)

            def y_hi(pair):
                act.wait_ge(pv_done, PER_PAIR * (pair + 1))
                dst = (yA_hi if pair < PAIRS else yB_hi)[:, pair % PAIRS, :]
                nc.scalar.activation(dst, y_bank, ACT.Copy).then_inc(y_hi_done, 1)

            act.wait_ge(sink_in, 16)
            for s in range(NS + LAG_PV):
                if s < NS:
                    exps(s)
                if 1 <= s <= NS // 2:
                    normalise(s - 1)
                if 0 <= s - LAG_T < NS:
                    copy_pt(s - LAG_T)
                if s >= LAG_PV and (s - LAG_PV) % PER_PAIR == PER_PAIR - 1:
                    y_hi((s - LAG_PV) // PER_PAIR)
                if s < NS and s % 4 == 3:
                    hi(0, U_GATES + s // 4 + 2)

            def sigmoids(m):
                for gt in (m, DT + m):
                    if m == 0:
                        act.wait_ge(proj_done, N_PROJ + N_GATES + 1)
                    nc.scalar.activation(gates[:, gt, :], gates[:, gt, :], ACT.Sigmoid).then_inc(gate_sig, 1)

            sigmoids(0)
            for m in range(DT):
                hi(0, U_BRANCH + m + 2)
                act.wait_ge(mix_done, m + 1)
                nc.scalar.activation(mix_hi[:, m, :], br[:, 0, :], ACT.Copy).then_inc(mix_hi_done, 1)
                if m + 1 < DT:
                    sigmoids(m + 1)
            for m in range(DT):
                hi(0, U_MIXOUT + m + 2)
                act.wait_ge(h_done, DT + m + 1)
                prepare(2, m)
            ffn_in(U_FFN2_IN, FT, 2)
            ffn_out(U_FFN2_OUT, 2 * DT, 3)

            act.wait_ge(p_in, 16)
            for j in range(PLE_T):
                nc.scalar.activation(p_hi[:, j, :], p_raw[:, j, :], ACT.Copy).then_inc(p_hi_done, 1)
            root(3)
            hi(0, U_PLE + 2)
            take_r(3)
            nc.scalar.activation(unused[:], ones[:], ACT.Sigmoid)
            for m in range(DT):
                act.wait_ge(pg_val_done, m + 1)
                nc.scalar.activation(pg_sig[:, m % 2, :], pg_val[:, m % 2, :], ACT.Sigmoid).then_inc(pg_sig_done, 1)
                if m:
                    hi(0, U_PLE + m + 2)
                act.wait_ge(h_done, 3 * DT + m + 1)
                squared(4, m)
            root(4)

        @block.vector
        def _(dve):
            def add_squares(k, m, slot=None):
                slot = m % 2 if slot is None else slot
                if isinstance(m, int) and m == 0:
                    return
                dve.wait_ge(sq_done, m + (DT * k + 1))
                if not (isinstance(m, int) and m < 2):
                    dve.wait_ge(sumsq_done, m + (7 * k - 1))
                nc.vector.tensor_tensor(sumsq[:], sumsq[:], squares[:, slot, :], ALU.add).then_inc(sumsq_done, 1)

            def x_part(k, m):
                dve.wait_ge(x_hi_done, m + (DT * k + 1))
                nc.vector.scalar_tensor_tensor(tile(x_lo, m), tile(h, m), gain(k, m), tile(x_hi, m).bitcast(F32),
                                               ALU.mult, ALU.subtract).then_inc(x_lo_done, 1)

            def prepare(k, m):
                x_part(k, m)
                add_squares(k, m)

            def norm(k):
                dve.wait_ge(std_done, k + 1)
                nc.vector.reciprocal(rstd[:], std[:]).then_inc(rstd_done, 1)
                dve.wait_ge(rstd_done, k + 1)
                nc.vector.tensor_copy(rstd_wide[:], rstd[:].unsqueeze(2).broadcast_to([P, NB, P])).then_inc(wide_done, 1)
                dve.wait_ge(r_done, k + 1)

            def ffn_in(u0, t0, k):
                def a_part(i, c, r):
                    t = t0 + r
                    dve.wait_ge(unit_done, 4 * i + (c + 1))
                    nc.vector.tensor_tensor(a_val[:, t % 2, :], acc[:, (2 * r + k) % 4, :], R[:], ALU.mult).then_inc(a_done, 1)

                def b_part(i, c, r):
                    t = t0 + r
                    now = 2 * i + (t + 1)
                    dve.wait_ge(unit_done, 4 * i + (c + 1))
                    nc.vector.tensor_tensor(ab[:, t % 2, :], acc[:, (2 * r + k) % 4 + 1, :], R[:], ALU.mult).then_inc(b_done, 1)
                    dve.wait_ge(b_done, now)
                    nc.vector.tensor_tensor(ab[:, t % 2, :], ab[:, t % 2, :], a_val[:, t % 2, :], ALU.mult).then_inc(ab_done, 1)
                    dve.wait_ge(ab_done, now)
                    dve.wait_ge(sig_done, now)
                    nc.vector.tensor_tensor(ab[:, t % 2, :], ab[:, t % 2, :], a_sig[:, t % 2, :], ALU.mult).then_inc(g_done, 1)
                    dve.wait_ge(g_hi_done, now)
                    j = 2 * i + r
                    nc.vector.tensor_tensor(tile(g_lo, j), ab[:, t % 2, :], tile(g_hi, j).bitcast(F32),
                                            ALU.subtract).then_inc(g_lo_done, 1)

                norm(k)
                with dve.Fori(0, FT // 2) as i:
                    for r in range(2):
                        a_part(i, u0 + 2 * r, r)
                        b_part(i, u0 + 2 * r + 1, r)

            def ffn_out(u0, h0, k):
                def pair_of_tiles(i, c):
                    for r in range(2):
                        m = 2 * i + (c - u0) // 2 + r
                        dve.wait_ge(unit_done, 4 * i + (c + 2 * r + 2))
                        nc.vector.scalar_tensor_tensor(tile(h, m), acc[:, k - 1 + r, :], 0.5, tile(h, m),
                                                       ALU.mult, ALU.add).then_inc(h_done, 1)
                        x_part(k, m)
                        add_squares(k, m, r)

                groups(dve, u0, 2 * DT, pair_of_tiles)

            dve.wait_ge(hi_done, 1)
            w = slice(0, K_IN * P)
            nc.vector.tensor_tensor(w_lo[:, 0, w], raw[:, 0, w], w_hi[:, 0, w].bitcast(F32),
                                    ALU.subtract).then_inc(lo_done, 1)
            for m in range(DT):
                x_part(0, m)
            for m in range(DT):
                add_squares(0, m)
            ffn_in(U_FFN1_IN, 0, 0)
            ffn_out(U_FFN1_OUT, 0, 1)
            norm(1)

            def bank(a):
                return acc[:, (a + 2) % 4, :]

            def query(dst, u, a):
                dve.wait_ge(unit_done, U_PROJ + u + 1)
                nc.vector.scalar_tensor_tensor(dst, bank(a), HD ** -0.5, R[:], ALU.mult, ALU.mult).then_inc(proj_done, 1)

            def scaled(dst, u, a):
                dve.wait_ge(unit_done, U_PROJ + u + 1)
                nc.vector.tensor_tensor(dst, bank(a), R[:], ALU.mult).then_inc(proj_done, 1)

            def keys_ib(u, a):
                dve.wait_ge(unit_done, U_PROJ + u + 1)
                for dst, half in ((kI, slice(0, HD)), (kB, slice(HD, P))):
                    nc.vector.tensor_tensor(dst[half, :], bank(a)[half, :], R[half, :], ALU.mult).then_inc(proj_done, 1)

            def values_b():
                src = att[:, 3, 0:NB * BVW].rearrange("p (n c) -> p n c", n=NB)
                dve.wait_ge(v_full, 1)
                nc.vector.tensor_scalar(w_idx[:], src[:, :, HD:BVW], HEADS ** -0.5, None, ALU.mult).then_inc(w_idx_done, 1)
                nc.vector.tensor_copy(vB[:], src[:, :, 0:HD]).then_inc(v_done, 1)

            def values_a():
                dve.wait_ge(v_full, 2)
                nc.vector.tensor_copy(vA[:], att[:, 3, :].rearrange("p (n c) -> p n c", n=NB)).then_inc(v_done, 1)

            def add_index(t):
                n, hh = INDEX[t]
                width = (n + 1) * P
                out = score[:, score_at[n]:score_at[n] + width]
                if t == 0:
                    dve.wait_ge(w_idx_done, 1)
                    dve.wait_ge(masks_done, 6)
                dve.wait_ge(relu_done, t + 1)
                if hh:
                    dve.wait_ge(idx_added, t)
                nc.vector.scalar_tensor_tensor(out, probs[:, t % 2, 0:width], w_idx[:, n, hh:hh + 1],
                                               out if hh else causal[:, T - width:T], ALU.mult, ALU.add).then_inc(idx_added, 1)

            rounds = list(enumerate(ROUNDS))

            def select(count):
                for r, (n, k) in [rounds.pop(0) for _ in range(min(count, len(rounds)))]:
                    width = (n + 1) * P
                    sc = score[:, score_at[n]:score_at[n] + width]
                    left = taken[:, 0:width]
                    src = left if k else sc
                    if k:
                        dve.wait_ge(took8, r)
                    elif r:
                        dve.wait_ge(mask_done, 3 - n)
                    else:
                        dve.wait_ge(idx_added, len(INDEX))
                    nc.vector.max(top8[:], src).then_inc(top8_done, 1)
                    dve.wait_ge(top8_done, r + 1)
                    nc.vector.match_replace(left, top8[:], src, TAKEN).then_inc(took8, 1)
                    if k == TOPK // 8 - 1:
                        dve.wait_ge(took8, r + 1)
                        nc.vector.tensor_tensor(sc, left, sc, ALU.is_equal).then_inc(untaken_done, 1)
                        dve.wait_ge(untaken_done, 4 - n)
                        nc.vector.tensor_scalar(sc, sc, NEG, None, ALU.mult).then_inc(mask_done, 1)

            for u in range(N_PROJ):
                if u == IBK:
                    keys_ib(u, u)
                elif u == BVIW:
                    dve.wait_ge(unit_done, U_PROJ + u + 1)
                    nc.vector.tensor_tensor(bvT[0:BVW, :], bank(u)[0:BVW, :], R[0:BVW, :], ALU.mult).then_inc(proj_done, 1)
                elif u == AV:
                    scaled(avT, u, u)
                elif u == AK:
                    scaled(kA[:], u, u)
                else:
                    q, first = (qI, IQ) if u < BQ else (qB, BQ) if u < AV else (qA, AQ)
                    query(q[:, u - first, :], u, u)
                if u == IQ + 1:
                    values_b()
                if BQ - 1 <= u < BQ + 2:
                    for t in range(HEADS * (u - BQ + 1), HEADS * (u - BQ + 2)):
                        add_index(t)
                elif u == BQ + 2:
                    for hh in range(HEADS):
                        nc.vector.scalar_tensor_tensor(biasA[:, 2 * (hh % 4) + hh // 4, :], dist[:, 2 * P:T], -SLOPES[hh],
                                                       window[:], ALU.mult, ALU.add).then_inc(biasA_done, 1)
                elif u > BQ + 2:
                    select(3)
                if u == AQ + 1:
                    values_a()

            def logits(s):
                kind, n, i, g = STEPS[s]
                head = i + 4 * g
                width = keys_of(kind, n)[1] * P
                w = slice(0, width)
                c = slice(s % 4, s % 4 + 1)
                if kind == "A":
                    bias = biasA[:, 2 * i + g, 2 * P - width:2 * P]
                else:
                    b = s - NS // 2
                    mask = score[:, score_at[n]:score_at[n] + width] if n else causal[:, T - P:T]
                    bias = biasB[:, s % 2, w]
                    if b >= 2:
                        dve.wait_ge(logits_done, s - 1)
                    nc.vector.scalar_tensor_tensor(bias, dist[:, T - width:T], -SLOPES[HEADS + head], mask,
                                                   ALU.mult, ALU.add).then_inc(biasB_done, 1)
                    dve.wait_ge(biasB_done, b + 1)
                dve.wait_ge(s_full, s + 1)
                if s >= 4:
                    dve.wait_ge(pt_full, s - 3)
                if s == 0:
                    dve.wait_ge(biasA_done, HEADS)
                nc.vector.tensor_tensor_reduce(out=probs[:, s % 4, w], in0=att[:, s % 2, w], in1=bias, scale=1.0,
                                               scalar=-3.4e38, op0=ALU.add, op1=ALU.max,
                                               accum_out=row_max[:, c]).then_inc(logits_done, 1)
                dve.wait_ge(logits_done, s + 1)
                if kind == "A":
                    nc.vector.tensor_scalar(neg_max[:, c], row_max[:, c], sink[:, head:head + 1], -1.0,
                                            ALU.max, ALU.mult).then_inc(neg_max_done, 1)
                else:
                    nc.vector.tensor_scalar(neg_max[:, c], row_max[:, c], -1.0, None, ALU.mult).then_inc(neg_max_done, 1)

            def normalise(s):
                kind, n, i, g = STEPS[s]
                w = slice(0, keys_of(kind, n)[1] * P)
                c = slice(s % 4, s % 4 + 1)
                dve.wait_ge(exp_done, s + 1)
                if kind == "A":
                    dve.wait_ge(sink_exp_done, s + 1)
                    nc.vector.tensor_tensor(row_sum[:, c], row_sum[:, c], sink_exp[:, c], ALU.add).then_inc(sum_done, 1)
                    dve.wait_ge(sum_done, s + 1)
                nc.vector.reciprocal(row_rcp[:, c], row_sum[:, c]).then_inc(rcp_done, 1)
                if kind == "A":
                    return
                dve.wait_ge(rcp_done, s + 1)
                nc.vector.tensor_scalar(probs[:, s % 4, w], probs[:, s % 4, w], row_rcp[:, c], None,
                                        ALU.mult).then_inc(probs_done, 1)

            def y_lo(pair):
                dst, hi_ = (yA_lo, yA_hi) if pair < PAIRS else (yB_lo, yB_hi)
                i = pair % PAIRS
                dve.wait_ge(y_hi_done, pair + 1)
                nc.vector.tensor_tensor(dst[:, i, :], y_bank, hi_[:, i, :].bitcast(F32), ALU.subtract).then_inc(y_lo_done, 1)

            dve.wait_ge(sink_in, 16)
            for s in range(NS + LAG_PV):
                if s < NS:
                    logits(s)
                if 1 <= s <= NS:
                    normalise(s - 1)
                if 2 <= s < NS // 2:
                    select(1)
                if s == NS // 2 - 1:
                    select(len(rounds))
                if s >= LAG_PV and (s - LAG_PV) % PER_PAIR == PER_PAIR - 1:
                    y_lo((s - LAG_PV) // PER_PAIR)
                if s % 4 == 0 and 0 < s <= NS:
                    gt = s // 4 - 1
                    scaled(gates[:, gt, :], N_PROJ + gt, N_PROJ + gt)

            for m in range(DT):
                pair = (2 * m + 2) % 4
                dve.wait_ge(unit_done, U_BRANCH + m + 1)
                dve.wait_ge(gate_sig, 2 * m + 2)
                if m:
                    dve.wait_ge(mix_lo_done, m)
                nc.vector.tensor_tensor(br[:, 0, :], acc[:, pair, :], gates[:, m, :], ALU.mult).then_inc(br_a, 1)
                nc.vector.tensor_tensor(br[:, 1, :], acc[:, pair + 1, :], gates[:, DT + m, :], ALU.mult).then_inc(br_b, 1)
                dve.wait_ge(br_b, m + 1)
                nc.vector.tensor_tensor(br[:, 0, :], br[:, 0, :], br[:, 1, :], ALU.add).then_inc(mix_done, 1)
                dve.wait_ge(mix_hi_done, m + 1)
                nc.vector.tensor_tensor(mix_lo[:, m, :], br[:, 0, :], mix_hi[:, m, :].bitcast(F32),
                                        ALU.subtract).then_inc(mix_lo_done, 1)
            for m in range(DT):
                dve.wait_ge(unit_done, U_MIXOUT + m + 1)
                nc.vector.tensor_tensor(h[:, m, :], acc[:, (m + 2) % 4, :], h[:, m, :], ALU.add).then_inc(h_done, 1)
                prepare(2, m)
            ffn_in(U_FFN2_IN, FT, 2)
            ffn_out(U_FFN2_OUT, 2 * DT, 3)

            for j in range(PLE_T):
                dve.wait_ge(p_hi_done, j + 1)
                nc.vector.tensor_tensor(p_lo[:, j, :], p_raw[:, j, :], p_hi[:, j, :].bitcast(F32),
                                        ALU.subtract).then_inc(p_lo_done, 1)
            norm(3)
            for m in range(DT):
                b = (2 * m) % 4
                dve.wait_ge(pg_full, m + 1)
                nc.vector.tensor_tensor(pg_val[:, m % 2, :], acc[:, b, :], R[:], ALU.mult).then_inc(pg_val_done, 1)
                dve.wait_ge(unit_done, U_PLE + m + 1)
                dve.wait_ge(pg_sig_done, m + 1)
                nc.vector.tensor_tensor(pg_val[:, m % 2, :], acc[:, b + 1, :], pg_sig[:, m % 2, :],
                                        ALU.mult).then_inc(pg_mul, 1)
                dve.wait_ge(pg_mul, m + 1)
                nc.vector.tensor_tensor(h[:, m, :], h[:, m, :], pg_val[:, m % 2, :], ALU.add).then_inc(h_done, 1)
                add_squares(4, m)

            dve.wait_ge(std_done, 5)
            nc.vector.reciprocal(rstd[:], std[:]).then_inc(rstd_done, 1)
            dve.wait_ge(rstd_done, 5)
            nc.vector.tensor_copy(rstd_wide[:], rstd[:].unsqueeze(2).broadcast_to([P, NB, P])).then_inc(wide_done, 1)
            dve.wait_ge(r_full, 5)
            for m in range(DT):
                nc.vector.scalar_tensor_tensor(result[:, m, :], h[:, m, :], gains[:, 4, m:m + 1], r_bank,
                                               ALU.mult, ALU.mult).then_inc(result_done, 1)

        @block.tensor
        def _(pe):
            mm = nc.tensor.matmul

            def wait_unit(i, c):
                pe.wait_ge(lo_done, 4 * i + (c + 1))

            def product(out, c, b, m_hi, m_lo, start, stop):
                w = slice(b * P, b * P + P)
                mm(out, w_hi[:, c % SPLIT, w], m_hi, start=start, stop=False)
                mm(out, w_hi[:, c % SPLIT, w], m_lo, start=False, stop=False)
                return mm(out, w_lo[:, c % SPLIT, w], m_hi, start=False, stop=stop)

            def x_unit(i, c, out, x0=None, midway=None):
                wait_unit(i, c)
                for b in range(DT):
                    if midway and b == DT // 2:
                        midway()
                    if x0 is not None:
                        pe.wait_ge(x_lo_done, x0 + b + 1)
                    last = product(out, c, b, x_hi[:, b, :], x_lo[:, b, :], b == 0, b == DT - 1)
                last.then_inc(unit_done, 1)

            def stats(k):
                pe.wait_ge(sumsq_done, 7 * (k + 1))
                for n in range(NB):
                    last = mm(stat_bank[:, n:n + 1], sumsq[:, n * P:(n + 1) * P], ones[:, 0:1], start=True, stop=True)
                last.then_inc(stat_done, 1)

            def spread(k):
                pe.wait_ge(wide_done, k + 1)
                for n in range(NB):
                    last = mm(r_bank[:, n * P:(n + 1) * P], rstd_wide[:, n, :], ident[:], start=True, stop=True)
                last.then_inc(r_full, 1)

            def ffn_in(u0, t0, k):
                for r in range(4):
                    if t0 and r == 0:
                        pe.wait_ge(h_done, 2 * DT - 2)
                    if t0 and r == 2:
                        pe.wait_ge(h_done, 2 * DT)
                    midway = {1: lambda: spread(k)} if k else {1: lambda: stats(k), 2: lambda: spread(k)}
                    x_unit(0, u0 + r, acc[:, (r + k) % 4, :], DT * k if r == 0 else None, midway.get(r))
                    if r == 0 and k:
                        stats(k)
                with pe.Fori(1, FT // 2) as i:
                    for r in range(4):
                        if r % 2 == 0:
                            pe.wait_ge(b_done, 2 * i + (t0 + r // 2 - 1))
                        x_unit(i, u0 + r, acc[:, (r + k) % 4, :])

            def ffn_out(u0, t0, h0):
                def pair_of_tiles(i, c):
                    first = isinstance(i, int) and c == u0
                    for r in range(2):
                        out = acc[:, r + (2 if t0 else 0), :]
                        if first:
                            pe.wait_ge(b_done, t0 + FT - 1)
                        else:
                            m = 2 * i + (c - u0) // 2 + r
                            pe.wait_ge(h_done, m + (h0 - 1))
                        for half in range(2):
                            u = c + 2 * r + half
                            wait_unit(i, u)
                            for b in range(K_OUT):
                                j = half * K_OUT + b
                                if first and r == 0:
                                    pe.wait_ge(g_lo_done, t0 + j + 1)
                                last = product(out, u, b, g_hi[:, j, :], g_lo[:, j, :], j == 0, j == FT - 1)
                            last.then_inc(unit_done, 1)

                pair_of_tiles(0, u0)
                with pe.Fori(1, DT // 2) as i:
                    pair_of_tiles(i, u0)

            pe.wait_ge(consts_done, 4)
            ffn_in(U_FFN1_IN, 0, 0)
            ffn_out(U_FFN1_OUT, 0, 0)

            def bank(a):
                return acc[:, (a + 2) % 4, :]

            def bank_free(a):
                if a in (2, 3):
                    pe.wait_ge(h_done, DT - 3 + a)
                elif a >= 4:
                    pe.wait_ge(proj_done, a - 2)

            def transpose_values(vT, width, number):
                for n in range(NB):
                    last = nc.tensor.transpose(att[:, 3, n * width:(n + 1) * width], vT[0:width, n * P:(n + 1) * P],
                                               ident[0:width, 0:width])
                last.then_inc(v_full, 1)

            def index_products(n):
                for hh in range(HEADS):
                    t = INDEX.index((n, hh))
                    half = slice(HD * (hh // 4), HD * (hh // 4) + HD)
                    if t == 0:
                        pe.wait_ge(proj_done, IQ + PAIRS + 1)
                        pe.wait_ge(k_copied, 32)
                    if t == 3:
                        pe.wait_ge(v_done, 1)
                    if t >= 4:
                        pe.wait_ge(relu_done, t - 3)
                    mm(att[:, t % 4, 0:(n + 1) * P], qI[half, hh % 4, n * P:(n + 1) * P], kI[half, 0:(n + 1) * P],
                       start=True, stop=True).then_inc(idx_full, 1)

            def values_b():
                pe.wait_ge(proj_done, BVIW + 2)
                transpose_values(bvT, BVW, 0)

            def values_a():
                pe.wait_ge(proj_done, AV + 2)
                pe.wait_ge(relu_done, len(INDEX))
                transpose_values(avT, P, 1)

            midway = {BVIW: lambda: spread(1), IQ + 1: values_b, BQ: lambda: index_products(3),
                      BQ + 1: lambda: index_products(2), BQ + 2: lambda: index_products(1), AQ + 1: values_a}
            for u in range(N_PROJ):
                bank_free(u)
                x_unit(0, U_PROJ + u, bank(u), DT if u == 0 else None, midway.get(u))
                if u == 0:
                    stats(1)

            def scores(s):
                kind, n, i, g = STEPS[s]
                first, count = keys_of(kind, n)
                half = slice(HD * g, HD * g + HD)
                q, k_ = (qA, kA) if kind == "A" else (qB, kB)
                if s == 0:
                    pe.wait_ge(proj_done, N_PROJ + 1)
                    pe.wait_ge(v_done, 2)
                if s >= 2:
                    pe.wait_ge(logits_done, s - 1)
                mm(att[:, s % 2, 0:count * P], q[half, i, n * P:(n + 1) * P], k_[half, first * P:(first + count) * P],
                   start=True, stop=True).then_inc(s_full, 1)

            def transposes(s):
                kind, n, i, g = STEPS[s]
                pe.wait_ge(probs_done, s + 1)
                if s >= 1:
                    pe.wait_ge(pt_copied, s)
                for b in range(keys_of(kind, n)[1]):
                    w = slice(b * P, (b + 1) * P)
                    last = nc.tensor.transpose(pt_bank[:, w], probs[:, s % 4, w], ident[:])
                last.then_inc(pt_full, 1)

            def weighted(s):
                kind, n, i, g = STEPS[s]
                first, count = keys_of(kind, n)
                half = slice(HD * g, HD * g + HD)
                pe.wait_ge(pt_copied, s + 1)
                if s % PER_PAIR == 0 and s:
                    pe.wait_ge(y_lo_done, s // PER_PAIR)
                for b in range(count):
                    v = vA[:, first + b, half] if kind == "A" else vB[:, first + b, :]
                    last = mm(y_bank[half, n * P:(n + 1) * P], v, probsT[:, s % 2, b * P:(b + 1) * P],
                              start=(b == 0), stop=(b == count - 1))
                last.then_inc(pv_done, 1)

            for s in range(NS + LAG_PV):
                if s < NS:
                    scores(s)
                if LAG_T <= s < NS + LAG_T:
                    transposes(s - LAG_T)
                if s < NS:
                    gt, quarter = divmod(s, 4)
                    c = U_GATES + gt
                    if quarter == 0:
                        bank_free(N_PROJ + gt)
                        wait_unit(0, c)
                    for b in (2 * quarter, 2 * quarter + 1):
                        last = product(bank(N_PROJ + gt), c, b, x_hi[:, b, :], x_lo[:, b, :], b == 0, b == DT - 1)
                    if quarter == 3:
                        last.then_inc(unit_done, 1)
                if s >= LAG_PV:
                    weighted(s - LAG_PV)

            for m in range(DT):
                pair = (2 * m + 2) % 4
                c = U_BRANCH + m
                if m < 2:
                    pe.wait_ge(proj_done, N_PROJ + N_GATES + m)
                else:
                    pe.wait_ge(br_b, m - 1)
                wait_unit(0, c)
                for b in range(2 * PAIRS):
                    y_h, y_l = (yA_hi, yA_lo) if b < PAIRS else (yB_hi, yB_lo)
                    i = b % PAIRS
                    if m == 0:
                        pe.wait_ge(y_lo_done, b + 1)
                    last = product(acc[:, pair + b // PAIRS, :], c, b, y_h[:, i, :], y_l[:, i, :],
                                   i == 0, i == PAIRS - 1)
                last.then_inc(unit_done, 1)
            for m in range(DT):
                c = U_MIXOUT + m
                if m < 4:
                    pe.wait_ge(br_b, DT - 1 + m // 2)
                else:
                    pe.wait_ge(h_done, DT + m - 3)
                wait_unit(0, c)
                for b in range(DT):
                    if m == 0:
                        pe.wait_ge(mix_lo_done, b + 1)
                    last = product(acc[:, (m + 2) % 4, :], c, b, mix_hi[:, b, :], mix_lo[:, b, :], b == 0, b == DT - 1)
                last.then_inc(unit_done, 1)

            ffn_in(U_FFN2_IN, FT, 2)
            ffn_out(U_FFN2_OUT, FT, 2 * DT)

            for m in range(DT):
                b0 = (2 * m) % 4
                c = U_PLE + m
                if m == 1:
                    pe.wait_ge(h_done, 3 * DT)
                if m >= 2:
                    pe.wait_ge(pg_mul, m - 1)
                wait_unit(0, c)
                for b in range(DT):
                    if m == 0:
                        pe.wait_ge(x_lo_done, 3 * DT + b + 1)
                    if m == 1 and b == DT // 2:
                        spread(3)
                    last = product(acc[:, b0, :], c, b, x_hi[:, b, :], x_lo[:, b, :], b == 0, b == DT - 1)
                last.then_inc(pg_full, 1)
                if m == 0:
                    stats(3)
                    pe.wait_ge(p_lo_done, PLE_T)
                for j in range(PLE_T):
                    last = product(acc[:, b0 + 1, :], c, DT + j, p_hi[:, j, :], p_lo[:, j, :], j == 0, j == PLE_T - 1)
                last.then_inc(unit_done, 1)
            stats(4)
            spread(4)


def _columns(w, cols, width=P):
    k = w.shape[0] // P
    out = np.zeros((len(cols), P, k, P), w.dtype)
    for n, c in enumerate(cols):
        out[n, :, :, 0:len(c)] = w[:, c].reshape(k, P, len(c)).transpose(1, 0, 2)
    return out.reshape(len(cols), P, k * P)


def kernel(**inputs):
    import concourse.bacc as bacc
    from concourse.bass_utils import run_bass_kernel_spmd

    a = {n: np.asarray(v) for n, v in inputs.items()}
    tiles = [np.arange(m * P, (m + 1) * P) for m in range(DT)]

    def feature_major(x):
        return np.ascontiguousarray(x.T.reshape(-1, P, T).transpose(1, 0, 2))

    def ffn_in(w):
        return _columns(w, [np.arange(s * FF + j * P, s * FF + (j + 1) * P) for j in range(FT) for s in range(2)])

    def ffn_out(w):
        u = _columns(w, tiles).reshape(DT, P, 2, K_OUT * P)
        return np.ascontiguousarray(u.transpose(0, 2, 1, 3)).reshape(2 * DT, P, K_OUT * P)

    sizes = dict(aq=512, ak=128, av=128, bq=512, bk=64, bv=64, iq=512, ik=64, iw=8, ga=D, gb=D)
    at, n = {}, 0
    for name, size in sizes.items():
        at[name] = n + np.arange(size)
        n += size
    pair = [np.concatenate([np.arange(i * HD, (i + 1) * HD), np.arange((i + 4) * HD, (i + 5) * HD)])
            for i in range(PAIRS)]
    proj = ([np.concatenate([at["ik"], at["bk"]]), np.concatenate([at["bv"], at["iw"]])]
            + [at["iq"][c] for c in pair] + [at["bq"][c] for c in pair] + [at["av"]]
            + [at["aq"][c] for c in pair] + [at["ak"]])
    gate = [at[s][c] for s in ("ga", "gb") for c in tiles]
    rows = np.concatenate(pair)
    branches = np.concatenate([_columns(a["w_br_a"][0][rows], tiles), _columns(a["w_br_b"][0][rows], tiles)], axis=2)
    mid = np.concatenate([_columns(a["w_in"][0], proj + gate), branches, _columns(a["w_out"][0], tiles)])
    ple = np.concatenate([_columns(a["w_ple_gate"][0], tiles), _columns(a["w_ple_proj"][0], tiles)], axis=2)
    gains = np.stack([a["ln_ffn1"][0], a["ln_mix"][0], a["ln_ffn2"][0], a["ln_ple"][0], a["ln_final"]])

    arrays = {
        "x": feature_major(a["x"][0]),
        "p": feature_major(a["p"][0, 0]),
        "gains": np.ascontiguousarray(gains.reshape(5, DT, P).transpose(2, 0, 1)),
        "sink": np.ascontiguousarray(np.broadcast_to(a["a_sink"][0], (P, HEADS))),
        "w_ffn1_in": ffn_in(a["w_ffn1_in"][0]),
        "w_ffn1_out": ffn_out(a["w_ffn1_out"][0]),
        "w_mid": mid,
        "w_ffn2_in": ffn_in(a["w_ffn2_in"][0]),
        "w_ffn2_out": ffn_out(a["w_ffn2_out"][0]),
        "w_ple": ple,
    }
    nc = bacc.Bacc("TRN2", target_bir_lowering=False, num_devices=1)
    args = [nc.dram_tensor(f"in_{n}", v.shape, mybir.dt.from_np(v.dtype), kind="ExternalInput").ap()
            for n, v in arrays.items()]
    args.append(nc.dram_tensor("out_t", (DT, P, T), F32, kind="ExternalOutput").ap())
    layer(nc, *args)
    r = run_bass_kernel_spmd(nc, [{f"in_{n}": v for n, v in arrays.items()}], core_ids=[0])
    out = r.results[0]["out_t"]
    return np.ascontiguousarray(out.reshape(D, T).T).reshape(1, T, D)
```

```python
from contextlib import ExitStack

import numpy as np

import concourse.bass as bass
from concourse import mybir
from concourse.alu_op_type import AluOpType as ALU

ACT = mybir.ActivationFunctionType
F32 = mybir.dt.float32
F32R = mybir.dt.float32r

P = 128
T = 512
NB = T // P
D = 1024
DT = D // P
FF = 2816
FT = FF // P
HD = 64
HEADS = 8
PAIRS = HEADS // 2
TOPK = min(256, T // 4)
PLE_T = 256 // P
EPS = 1e-6
NEG = -1e30
TAKEN = -3.0e38
SLOPES = [float(s) for s in np.float32(2.0) ** (np.float32(-8.0) * np.arange(1, 17, dtype=np.float32) / np.float32(16))]

RAW = 4
SPLIT = 2
K_IN, K_OUT, K_PLE = DT, FT // 2, DT + PLE_T

U_FFN1_IN = 0
U_FFN1_OUT = U_FFN1_IN + 2 * FT
U_PROJ = U_FFN1_OUT + 2 * DT
(IBK, BVIW, IQ, BQ, AV, AQ, AK) = (0, 1, 2, 6, 10, 11, 15)
N_PROJ = 16
N_GATES = 2 * DT
U_GATES = U_PROJ + N_PROJ
U_BRANCH = U_GATES + N_GATES
U_MIXOUT = U_BRANCH + DT
U_FFN2_IN = U_MIXOUT + DT
U_FFN2_OUT = U_FFN2_IN + 2 * FT
U_PLE = U_FFN2_OUT + 2 * DT
U_END = U_PLE + DT
N_MID = U_FFN2_IN - U_PROJ
BVW = HD + HEADS

STEPS = [(kind, n, i, g) for kind in "AB" for i in range(PAIRS) for n in range(NB) for g in range(2)]
NS = len(STEPS)
RING = 5
LAG_T, LAG_PV = 4, 5
LAG_Y = 1
PER_PAIR = 2 * NB
INDEX = [(n, h) for n in (3, 2, 1) for h in range(HEADS)]
ROUNDS = [(n, k) for k in range(TOPK // 8) for n in (3, 2, 1)]
ROUNDS_IN_UNIT = 4
SELECT_FROM = 6
WARM_UP, WARM_GAP = 10, 5
HALVES = (slice(0, T // 2), slice(T // 2, T))


def unit_rows(u):
    if U_FFN1_OUT <= u < U_PROJ or U_FFN2_OUT <= u < U_PLE:
        return K_OUT
    return K_PLE if u >= U_PLE else K_IN


def layer(nc, x_d, p_d, gains_d, sink_d, w1i_d, w1o_d, wmid_d, w2i_d, w2o_d, wple_d, out_d):
    ctx = ExitStack()
    with ctx:
        def sb(name, shape, dt=F32):
            return ctx.enter_context(nc.sbuf_tensor(name, shape, dt))

        def sem(name):
            return ctx.enter_context(nc.semaphore(name))

        h = sb("h", [P, DT, T])
        x_hi = sb("x_hi", [P, DT, T], F32R)
        x_lo = sb("x_lo", [P, DT, T], F32R)
        raw = sb("raw", [P, RAW, K_OUT * P])
        w_hi = sb("w_hi", [P, SPLIT, K_OUT * P], F32R)
        w_lo = sb("w_lo", [P, SPLIT, K_OUT * P], F32R)
        R = sb("R", [P, T])
        squares = sb("squares", [P, 2, T])
        sumsq = sb("sumsq", [P, T])
        rstd_wide = sb("rstd_wide", [P, NB, P])
        std = sb("std", [P, NB])
        sum_last = sb("sum_last", [P, NB])
        rstd = sb("rstd", [P, NB])
        gains = sb("gains", [P, 5, DT])
        sink = sb("sink", [P, HEADS])
        ones = sb("ones", [P, 1])
        eps = sb("eps", [P, 1])
        ident = sb("ident", [P, P])
        row_max = sb("row_max", [P, RING])
        neg_max = sb("neg_max", [P, RING])
        row_sum = sb("row_sum", [P, RING])
        sink_exp = sb("sink_exp", [P, RING])
        row_rcp = sb("row_rcp", [P, RING])
        top8 = sb("top8", [P, 3, 8])
        unused = sb("unused", [P, 1])

        base = nc.sbuf_base
        base = (base + 31) // 32 * 32
        region = nc.sbuf_usable_end - base

        class Place:

            def __init__(self, at=0):
                self.at = at

            def __call__(self, name, shape, dt=F32):
                t = nc.alloc_sbuf_tensor_at(name, shape, dt, offset=base + self.at)
                self.at += 4 * int(np.prod(shape[1:]))
                self.at = (self.at + 31) // 32 * 32
                assert self.at <= region, (name, self.at, region)
                return t

        ffn = Place()
        g_hi = ffn("g_hi", [P, FT, T], F32R)
        g_lo = ffn("g_lo", [P, FT, T], F32R)
        ffn_work = ffn.at
        a_val = ffn("a_val", [P, 2, T])
        a_sig = ffn("a_sig", [P, 2, T])
        ab = ffn("ab", [P, 2, T])
        mid = Place()
        gates = mid("gates", [P, N_GATES, T])
        q_place = mid.at
        qA = mid("qA", [P, PAIRS, T])
        qB = mid("qB", [P, PAIRS, T])
        qI = mid("qI", [P, PAIRS, T])
        biasA = mid("biasA", [P, HEADS, 2 * P])
        over_q = Place(q_place)
        yA_hi = over_q("yA_hi", [P, PAIRS, T], F32R)
        yB_hi = over_q("yB_hi", [P, PAIRS, T], F32R)
        yB_lo = over_q("yB_lo", [P, PAIRS, T], F32R)
        yA_lo = over_q("yA_lo", [P, PAIRS, T], F32R)
        temps = mid.at
        kA = mid("kA", [P, T])
        kB = mid("kB", [P, T])
        kI = mid("kI", [P, T])
        vA = mid("vA", [P, NB, P])
        vB = mid("vB", [P, NB, HD])
        w_idx = mid("w_idx", [P, NB, HEADS])
        score_at = [None, 0, 2 * P, 5 * P]
        score = mid("score", [P, 9 * P])
        dist = mid("dist", [P, T])
        causal = mid("causal", [P, T])
        window = mid("window", [P, 2 * P])
        probs = mid("probs", [P, RING, T])
        biasB = mid("biasB", [P, 2, T])
        probsT = mid("probsT", [P, 2, T])
        bvT, avT = probs[:, 2, :], probs[:, 3, :]
        merge = Place(temps)
        mix_hi = merge("mix_hi", [P, DT, T], F32R)
        mix_lo = merge("mix_lo", [P, DT, T], F32R)
        br = merge("br", [P, 2, T])
        ple_p = Place(ffn_work)
        p_raw = ple_p("p_raw", [P, PLE_T, T])
        p_hi = ple_p("p_hi", [P, PLE_T, T], F32R)
        p_lo = ple_p("p_lo", [P, PLE_T, T], F32R)
        ple = Place()
        pg_val = ple("pg_val", [P, 2, T])
        pg_sig = ple("pg_sig", [P, 2, T])
        result = ple("result", [P, DT, T])

        acc = ctx.enter_context(nc.psum_tensor("acc", [P, 4, T], F32))
        att = ctx.enter_context(nc.psum_tensor("att", [P, 4, T], F32))
        stat_bank, r_bank = att[:, 3, 0:NB], att[:, 2, :]
        stat_bank_last = att[:, 1, 0:NB]
        pt_bank = att[:, 2, :]

        def s_bank(s):
            return acc[:, 0, :] if s % 3 == 2 else att[:, s % 3, :]

        def y_bank(pair):
            return acc[:, 1, :] if pair % 2 else att[:, 3, :]

        def gate_bank(gt):
            return acc[:, 2 + gt % 2, :]

        raw_in = [sem(f"raw_in{s}") for s in range(RAW)]
        x_in = [sem(f"x_in{m}") for m in range(DT)]
        gains_in, sink_in, p_in = sem("gains_in"), sem("sink_in"), sem("p_in")
        out_done = sem("out_done")
        consts_done = sem("consts_done")
        half_in = [sem(f"half_in{u}") for u in range(2)]
        half_hi_done = [sem(f"half_hi_done{u}") for u in range(2)]
        half_lo_done = [sem(f"half_lo_done{u}") for u in range(2)]
        first_half, second_half = slice(0, K_IN // 2 * P), slice(K_IN // 2 * P, K_IN * P)
        hi_done = sem("hi_done")
        lo_done = sem("lo_done")
        unit_done = sem("unit_done")
        x_hi_done, x_lo_done = sem("x_hi_done"), sem("x_lo_done")
        sq_done, sumsq_done = sem("sq_done"), sem("sumsq_done")
        stat_done, std_done, rstd_done = sem("stat_done"), sem("std_done"), sem("rstd_done")
        wide_done, r_full, r_done = sem("wide_done"), sem("r_full"), sem("r_done")
        h_done = sem("h_done")
        a_done, sig_done, b_done = sem("a_done"), sem("sig_done"), sem("b_done")
        ab_done, g_done = sem("ab_done"), sem("g_done")
        g_hi_done, g_lo_done = sem("g_hi_done"), sem("g_lo_done")
        proj_done = sem("proj_done")
        k_copied = sem("k_copied")
        v_full = sem("v_full")
        v_done, w_idx_done = sem("v_done"), sem("w_idx_done")
        masks_done = sem("masks_done")
        biasA_done = sem("biasA_done")
        idx_full, relu_done, idx_added = sem("idx_full"), sem("relu_done"), sem("idx_added")
        top8_done, took8 = sem("top8_done"), sem("took8")
        mask_done = sem("mask_done")
        s_full, biasB_done, logits_done = sem("s_full"), sem("biasB_done"), sem("logits_done")
        neg_max_done, exp_done, sink_exp_done = sem("neg_max_done"), sem("exp_done"), sem("sink_exp_done")
        sum_done, rcp_done, probs_done = sem("sum_done"), sem("rcp_done"), sem("probs_done")
        pt_full, pt_copied, pv_done = sem("pt_full"), sem("pt_copied"), sem("pv_done")
        y_hi_done, y_lo_done = sem("y_hi_done"), sem("y_lo_done")
        gate_sig = sem("gate_sig")
        br_a, br_b, mix_done = sem("br_a"), sem("br_b"), sem("mix_done")
        mix_hi_done, mix_lo_done = sem("mix_hi_done"), sem("mix_lo_done")
        p_hi_done, p_lo_done = sem("p_hi_done"), sem("p_lo_done")
        pg_full = sem("pg_full")
        pg_val_done, pg_sig_done, pg_mul = sem("pg_val_done"), sem("pg_sig_done"), sem("pg_mul")
        stat_first_done = sem("stat_first_done")
        sum_first_done, sum_last_done = sem("sum_first_done"), sem("sum_last_done")
        result_done = sem("result_done")

        block = ctx.enter_context(nc.Block())

        def keys_of(kind, n):
            first = max(n - 1, 0) if kind == "A" else 0
            return first, n + 1 - first

        def tile(t, j):
            return t[:, j, :] if isinstance(j, int) else t[:, bass.ds(j, 1), :].rearrange("p a c -> p (a c)")

        def gain(k, m):
            return gains[:, k, m:m + 1] if isinstance(m, int) else gains[:, k, bass.ds(m, 1)]

        def groups(eng, first_unit, n, body):
            last = n // 4 - 1
            body(0, first_unit)
            with eng.Fori(1, last) as i:
                body(i, first_unit)
            body(0, first_unit + 4 * last)

        @block.sync
        def _(sp):
            def load(w_d, i, c, first, rows):
                s = c % RAW
                if not (isinstance(i, int) and c + 4 * i < RAW):
                    sp.wait_ge(lo_done, 4 * i + (c - RAW + 1))
                n = 4 * i + (c - first)
                src = w_d[n] if isinstance(n, int) else w_d[bass.ds(n, 1), :, :].rearrange("u p c -> (u p) c")
                sp.dma_start(raw[:, s, 0:rows * P], src).then_inc(raw_in[s], 16)

            def loads(w_d, first, n, rows):
                with sp.Fori(1 if first == 0 else 0, n // 4) as i:
                    for r in range(4):
                        load(w_d, i, first + r, first, rows)

            def load_x(m):
                sp.dma_start(h[:, m, :], x_d[:, m, :]).then_inc(x_in[m], 16)

            def load_half(u, half, done):
                sp.dma_start(raw[:, u, half], w1i_d[u][:, half]).then_inc(done, 16)

            load_half(0, first_half, half_in[0])
            load_x(0)
            load_half(0, second_half, raw_in[0])
            for m in range(1, DT):
                load_x(m)
            load_half(1, first_half, half_in[1])
            load_half(1, second_half, raw_in[1])
            load(w1i_d, 0, 2, 0, K_IN)
            load(w1i_d, 0, 3, 0, K_IN)
            loads(w1i_d, U_FFN1_IN, 2 * FT, K_IN)
            loads(w1o_d, U_FFN1_OUT, 2 * DT, K_OUT)
            loads(wmid_d, U_PROJ, N_MID, K_IN)
            loads(w2i_d, U_FFN2_IN, 2 * FT, K_IN)
            loads(w2o_d, U_FFN2_OUT, 2 * DT, K_OUT)
            sp.wait_ge(g_lo_done, 2 * FT)
            sp.dma_start(p_raw[:], p_d).then_inc(p_in, 16)
            loads(wple_d, U_PLE, DT, K_PLE)
            for m in range(DT):
                sp.wait_ge(result_done, m + 1)
                sp.dma_start(out_d[m], result[:, m, :]).then_inc(out_done, 16)
            sp.wait_ge(out_done, 16 * DT)

        @block.gpsimd
        def _(pool):
            nc.gpsimd.memset(ones[:], 1.0).then_inc(consts_done, 1)
            nc.gpsimd.memset(ident[:], 0.0).then_inc(consts_done, 1)
            nc.gpsimd.memset(eps[:], EPS).then_inc(consts_done, 1)
            pool.wait_ge(consts_done, 3)
            nc.gpsimd.affine_select(out=ident[:], in_=ident[:], compare_op=ALU.not_equal, fill=1.0, base=0,
                                    pattern=[[-1, P]], channel_multiplier=1).then_inc(consts_done, 1)

            def lo(i, c, rows):
                w = slice(0, rows * P)
                pool.wait_ge(hi_done, 4 * i + (c + 1))
                nc.gpsimd.tensor_tensor(w_lo[:, c % SPLIT, w], raw[:, c % RAW, w],
                                        w_hi[:, c % SPLIT, w].bitcast(F32), ALU.subtract).then_inc(lo_done, 1)

            def los(first, n, rows, start=0):
                with pool.Fori(start, n // 4) as i:
                    for r in range(4):
                        lo(i, first + r, rows)

            pool.wait_ge(half_hi_done[1], 1)
            nc.gpsimd.tensor_tensor(w_lo[:, 1, first_half], raw[:, 1, first_half], w_hi[:, 1, first_half].bitcast(F32),
                                    ALU.subtract).then_inc(half_lo_done[1], 1)
            pool.wait_ge(hi_done, 2)
            pool.wait_ge(lo_done, 1)
            nc.gpsimd.tensor_tensor(w_lo[:, 1, second_half], raw[:, 1, second_half], w_hi[:, 1, second_half].bitcast(F32),
                                    ALU.subtract).then_inc(lo_done, 1)
            for c in range(2, 4):
                lo(0, c, K_IN)
            los(U_FFN1_IN, 2 * FT, K_IN, start=1)
            los(U_FFN1_OUT, 2 * DT, K_OUT)
            los(U_PROJ, 4, K_IN)
            nc.gpsimd.iota(dist[:], pattern=[[-1, T]], base=T - P, channel_multiplier=1,
                           allow_small_or_imprecise_dtypes=True).then_inc(masks_done, 1)
            nc.gpsimd.memset(causal[:], 0.0).then_inc(masks_done, 1)
            nc.gpsimd.memset(window[:], 0.0).then_inc(masks_done, 1)
            los(U_PROJ + 4, 4, K_IN)
            pool.wait_ge(masks_done, 3)
            nc.gpsimd.affine_select(out=causal[:], in_=causal[:], compare_op=ALU.is_ge, fill=NEG, base=T - P,
                                    pattern=[[-1, T]], channel_multiplier=1).then_inc(masks_done, 1)
            nc.gpsimd.affine_select(out=window[:], in_=window[:], compare_op=ALU.is_ge, fill=NEG, base=P,
                                    pattern=[[-1, 2 * P]], channel_multiplier=1).then_inc(masks_done, 1)
            pool.wait_ge(masks_done, 5)
            nc.gpsimd.affine_select(out=window[:], in_=window[:], compare_op=ALU.is_ge, fill=NEG, base=-1,
                                    pattern=[[1, 2 * P]], channel_multiplier=-1).then_inc(masks_done, 1)
            los(U_PROJ + 8, N_MID - 8, K_IN)
            los(U_FFN2_IN, 2 * FT, K_IN)
            los(U_FFN2_OUT, 2 * DT, K_OUT)
            los(U_PLE, DT, K_PLE)

        @block.scalar
        def _(act):
            def hi(i, c):
                if isinstance(i, int) and c + 4 * i >= U_END:
                    return
                w = slice(0, unit_rows(c) * P)
                act.wait_ge(raw_in[c % RAW], 16 * i + 16 * (c // RAW + 1))
                if not (isinstance(i, int) and c + 4 * i < SPLIT):
                    act.wait_ge(unit_done, 4 * i + (c - SPLIT + 1))
                nc.scalar.activation(w_hi[:, c % SPLIT, w], raw[:, c % RAW, w], ACT.Copy).then_inc(hi_done, 1)

            def squares_free(k, m):
                if not (isinstance(m, int) and m < 3):
                    act.wait_ge(sumsq_done, m + (7 * k - 2))

            def squared(k, m, slot=None, waits=True):
                slot = m % 2 if slot is None else slot
                first = isinstance(m, int) and m == 0
                if waits:
                    squares_free(k, m)
                nc.scalar.activation(sumsq[:] if first else squares[:, slot, :], tile(h, m),
                                     ACT.Square).then_inc(sq_done, 1)

            def x_part(k, m):
                nc.scalar.activation(tile(x_hi, m), tile(h, m), ACT.Copy,
                                     scale=gain(k, m)).then_inc(x_hi_done, 1)

            def prepare(k, m):
                x_part(k, m)
                squared(k, m)

            def root(k):
                act.wait_ge(stat_done, k + 1)
                nc.scalar.activation(std[:], stat_bank, ACT.Sqrt, bias=eps[:, 0:1],
                                     scale=1.0 / D).then_inc(std_done, 1)

            def take_r(k):
                act.wait_ge(r_full, k + 1)
                nc.scalar.activation(R[:], r_bank, ACT.Copy).then_inc(r_done, 1)

            def ffn_in(u0, t0, k):
                def sig(i, r):
                    t = t0 + r
                    act.wait_ge(a_done, 2 * i + (t + 1))
                    nc.scalar.activation(a_sig[:, t % 2, :], a_val[:, t % 2, :], ACT.Sigmoid).then_inc(sig_done, 1)

                def gated(i, r):
                    t = t0 + r
                    act.wait_ge(g_done, 2 * i + (t + 1))
                    j = 2 * i + r
                    nc.scalar.activation(tile(g_hi, j), ab[:, t % 2, :], ACT.Copy).then_inc(g_hi_done, 1)

                root(k)
                nc.scalar.activation(unused[:], ones[:], ACT.Sigmoid)
                if k:
                    hi(0, u0 + 2)
                    take_r(k)
                    hi(0, u0 + 3)
                else:
                    hi(0, u0 + 4)
                    take_r(k)
                sig(0, 0)
                if not k:
                    hi(0, u0 + 5)
                gated(0, 0)
                if k:
                    hi(0, u0 + 4)
                sig(0, 1)
                if k:
                    hi(0, u0 + 5)
                gated(0, 1)
                with act.Fori(1, FT // 2 - 1) as i:
                    for r in range(2):
                        hi(i, u0 + 2 * r + 2)
                        sig(i, r)
                        hi(i, u0 + 2 * r + 3)
                        gated(i, r)
                for r in range(2):
                    c = u0 + 2 * FT - 4 + 2 * r
                    hi(0, c + 2)
                    sig(FT // 2 - 1, r)
                    hi(0, c + 3)
                    gated(FT // 2 - 1, r)

            def ffn_out(u0, h0, k):
                def pair_of_tiles(i, c):
                    for r in range(2):
                        m = 2 * i + (c - u0) // 2 + r
                        hi(i, c + 2 * r + 2)
                        hi(i, c + 2 * r + 3)
                        squares_free(k, m)
                        act.wait_ge(h_done, m + (h0 + 1))
                        x_part(k, m)
                        squared(k, m, r, waits=False)

                groups(act, u0, 2 * DT, pair_of_tiles)

            act.wait_ge(consts_done, 1)
            nc.scalar.activation(unused[:], ones[:], ACT.Sqrt)
            act.dma_start(gains[:], gains_d).then_inc(gains_in, 16)
            act.dma_start(sink[:], sink_d).then_inc(sink_in, 16)
            act.wait_ge(consts_done, 4)
            def hi_first_half(u):
                act.wait_ge(half_in[u], 16)
                nc.scalar.activation(w_hi[:, u, first_half], raw[:, u, first_half], ACT.Copy).then_inc(half_hi_done[u], 1)

            def hi_second_half(u):
                act.wait_ge(raw_in[u], 16)
                nc.scalar.activation(w_hi[:, u, second_half], raw[:, u, second_half], ACT.Copy).then_inc(hi_done, 1)

            hi_first_half(0)
            act.wait_ge(gains_in, 16)
            for m in range(DT):
                act.wait_ge(x_in[m], 16)
                x_part(0, m)
                if m == 0:
                    hi_second_half(0)
            hi_first_half(1)
            hi_second_half(1)
            for m in range(DT):
                squared(0, m)
                if m == 2:
                    hi(0, 2)
                if m == DT - 2:
                    hi(0, 3)
            ffn_in(U_FFN1_IN, 0, 0)
            ffn_out(U_FFN1_OUT, 0, 1)

            u0 = U_PROJ
            root(1)
            hi(0, u0 + 2)
            take_r(1)
            hi(0, u0 + 3)

            def relu(t):
                n, _ = INDEX[t]
                w = slice(0, (n + 1) * P)
                act.wait_ge(idx_full, t + 1)
                if t >= 2:
                    act.wait_ge(idx_added, t - 1)
                nc.scalar.activation(probs[:, t % 2, w], att[:, t % 4, w], ACT.Relu).then_inc(relu_done, 1)

            for u in range(2, N_PROJ):
                if BQ <= u < BQ + 3:
                    for t in range(HEADS * (u - BQ), HEADS * (u - BQ + 1)):
                        relu(t)
                hi(0, u0 + u + 2)
                if u == 2:
                    act.wait_ge(proj_done, 2)
                    act.dma_start(kI[HD:P, :], kI[0:HD, :]).then_inc(k_copied, 16)
                    act.dma_start(kB[0:HD, :], kB[HD:P, :]).then_inc(k_copied, 16)
                if u == BQ + 3:
                    nc.scalar.activation(unused[:], ones[:], ACT.Exp)

            def exps(s):
                kind, n, i, g = STEPS[s]
                w = slice(0, keys_of(kind, n)[1] * P)
                head = i + 4 * g
                act.wait_ge(neg_max_done, s + 1)
                nc.scalar.activation(probs[:, s % RING, w], probs[:, s % RING, w], ACT.Exp, bias=neg_max[:, s % RING:s % RING + 1],
                                     accum_out=row_sum[:, s % RING:s % RING + 1]).then_inc(exp_done, 1)
                if kind == "A":
                    nc.scalar.activation(sink_exp[:, s % RING:s % RING + 1], neg_max[:, s % RING:s % RING + 1], ACT.Exp,
                                         bias=sink[:, head:head + 1]).then_inc(sink_exp_done, 1)

            def normalise(s):
                kind, n, i, g = STEPS[s]
                w = slice(0, keys_of(kind, n)[1] * P)
                act.wait_ge(rcp_done, s + 1)
                nc.scalar.activation(probs[:, s % RING, w], probs[:, s % RING, w], ACT.Copy,
                                     scale=row_rcp[:, s % RING:s % RING + 1]).then_inc(probs_done, 1)

            def copy_pt(s):
                kind, n, i, g = STEPS[s]
                w = slice(0, keys_of(kind, n)[1] * P)
                act.wait_ge(pt_full, s + 1)
                if s >= 2:
                    act.wait_ge(pv_done, s - 1)
                nc.scalar.activation(probsT[:, s % 2, w], pt_bank[:, w], ACT.Copy).then_inc(pt_copied, 1)

            def y_hi(pair):
                act.wait_ge(pv_done, PER_PAIR * (pair + 1))
                dst = (yA_hi if pair < PAIRS else yB_hi)[:, pair % PAIRS, :]
                nc.scalar.activation(dst, y_bank(pair), ACT.Copy).then_inc(y_hi_done, 1)

            act.wait_ge(sink_in, 16)
            for s in range(NS + LAG_PV + LAG_Y + 1):
                if s < NS:
                    exps(s)
                if 1 <= s <= NS // 2:
                    normalise(s - 1)
                if 0 <= s - LAG_T < NS:
                    copy_pt(s - LAG_T)
                if s - LAG_PV >= PER_PAIR and (s - LAG_PV - LAG_Y) % PER_PAIR == 0:
                    y_hi((s - LAG_PV - LAG_Y) // PER_PAIR - 1)
                if s > 4 and s % 4 == 1 and s < NS + 4:
                    hi(0, U_GATES + s // 4 + 1)

            def sigmoids(m):
                for gt in (m, DT + m):
                    if m == 0:
                        act.wait_ge(proj_done, N_PROJ + N_GATES + 1)
                    nc.scalar.activation(gates[:, gt, :], gates[:, gt, :], ACT.Sigmoid).then_inc(gate_sig, 1)

            sigmoids(0)
            for m in range(DT):
                hi(0, U_BRANCH + m + 2)
                act.wait_ge(mix_done, m + 1)
                nc.scalar.activation(mix_hi[:, m, :], br[:, 0, :], ACT.Copy).then_inc(mix_hi_done, 1)
                if m + 1 < DT:
                    sigmoids(m + 1)
            for m in range(DT):
                hi(0, U_MIXOUT + m + 2)
                act.wait_ge(h_done, DT + m + 1)
                prepare(2, m)
            ffn_in(U_FFN2_IN, FT, 2)
            ffn_out(U_FFN2_OUT, 2 * DT, 3)

            act.wait_ge(p_in, 16)
            for j in range(PLE_T):
                nc.scalar.activation(p_hi[:, j, :], p_raw[:, j, :], ACT.Copy).then_inc(p_hi_done, 1)
            root(3)
            hi(0, U_PLE + 2)
            take_r(3)
            nc.scalar.activation(unused[:], ones[:], ACT.Sigmoid)

            def ple_sigmoid(m, number, w):
                act.wait_ge(pg_val_done, number + 1)
                nc.scalar.activation(pg_sig[:, m % 2, w], pg_val[:, m % 2, w], ACT.Sigmoid).then_inc(pg_sig_done, 1)

            for m in range(DT - 1):
                ple_sigmoid(m, m, slice(0, T))
                if m:
                    hi(0, U_PLE + m + 2)
                act.wait_ge(h_done, 3 * DT + m + 1)
                squared(4, m)
            for part, w in enumerate(HALVES):
                ple_sigmoid(DT - 1, DT - 1 + part, w)
            nc.scalar.activation(unused[:], ones[:], ACT.Sqrt)
            squares_free(4, DT - 1)
            for part, w in enumerate(HALVES):
                act.wait_ge(h_done, 4 * DT + part)
                nc.scalar.activation(squares[:, (DT - 1) % 2, w], h[:, DT - 1, w], ACT.Square).then_inc(sq_done, 1)
            act.wait_ge(sum_last_done, 1)
            nc.scalar.activation(std[:], sum_last[:], ACT.Sqrt, bias=eps[:, 0:1], scale=1.0 / D).then_inc(std_done, 1)

        @block.vector
        def _(dve):
            def add_squares(k, m, slot=None):
                slot = m % 2 if slot is None else slot
                if isinstance(m, int) and m == 0:
                    return
                dve.wait_ge(sq_done, m + (DT * k + 1))
                if not (isinstance(m, int) and m < 2):
                    dve.wait_ge(sumsq_done, m + (7 * k - 1))
                nc.vector.tensor_tensor(sumsq[:], sumsq[:], squares[:, slot, :], ALU.add).then_inc(sumsq_done, 1)

            def x_part(k, m):
                dve.wait_ge(x_hi_done, m + (DT * k + 1))
                nc.vector.scalar_tensor_tensor(tile(x_lo, m), tile(h, m), gain(k, m), tile(x_hi, m).bitcast(F32),
                                               ALU.mult, ALU.subtract).then_inc(x_lo_done, 1)

            def prepare(k, m):
                x_part(k, m)
                add_squares(k, m)

            def norm(k):
                dve.wait_ge(std_done, k + 1)
                nc.vector.reciprocal(rstd[:], std[:]).then_inc(rstd_done, 1)
                dve.wait_ge(rstd_done, k + 1)
                nc.vector.tensor_copy(rstd_wide[:], rstd[:].unsqueeze(2).broadcast_to([P, NB, P])).then_inc(wide_done, 1)
                dve.wait_ge(r_done, k + 1)

            def ffn_in(u0, t0, k):
                def a_part(i, c, r):
                    t = t0 + r
                    dve.wait_ge(unit_done, 4 * i + (c + 1))
                    nc.vector.tensor_tensor(a_val[:, t % 2, :], acc[:, (2 * r + k) % 4, :], R[:], ALU.mult).then_inc(a_done, 1)

                def b_part(i, c, r):
                    t = t0 + r
                    now = 2 * i + (t + 1)
                    dve.wait_ge(unit_done, 4 * i + (c + 1))
                    nc.vector.tensor_tensor(ab[:, t % 2, :], acc[:, (2 * r + k) % 4 + 1, :], R[:], ALU.mult).then_inc(b_done, 1)
                    dve.wait_ge(b_done, now)
                    nc.vector.tensor_tensor(ab[:, t % 2, :], ab[:, t % 2, :], a_val[:, t % 2, :], ALU.mult).then_inc(ab_done, 1)
                    dve.wait_ge(ab_done, now)
                    dve.wait_ge(sig_done, now)
                    nc.vector.tensor_tensor(ab[:, t % 2, :], ab[:, t % 2, :], a_sig[:, t % 2, :], ALU.mult).then_inc(g_done, 1)
                    dve.wait_ge(g_hi_done, now)
                    j = 2 * i + r
                    nc.vector.tensor_tensor(tile(g_lo, j), ab[:, t % 2, :], tile(g_hi, j).bitcast(F32),
                                            ALU.subtract).then_inc(g_lo_done, 1)

                norm(k)
                with dve.Fori(0, FT // 2) as i:
                    for r in range(2):
                        a_part(i, u0 + 2 * r, r)
                        b_part(i, u0 + 2 * r + 1, r)

            def ffn_out(u0, h0, k):
                def pair_of_tiles(i, c):
                    for r in range(2):
                        m = 2 * i + (c - u0) // 2 + r
                        dve.wait_ge(unit_done, 4 * i + (c + 2 * r + 2))
                        nc.vector.scalar_tensor_tensor(tile(h, m), acc[:, k - 1 + r, :], 0.5, tile(h, m),
                                                       ALU.mult, ALU.add).then_inc(h_done, 1)
                        x_part(k, m)
                        add_squares(k, m, r)

                groups(dve, u0, 2 * DT, pair_of_tiles)

            dve.wait_ge(half_hi_done[0], 1)
            nc.vector.tensor_tensor(w_lo[:, 0, first_half], raw[:, 0, first_half], w_hi[:, 0, first_half].bitcast(F32),
                                    ALU.subtract).then_inc(half_lo_done[0], 1)
            x_part(0, 0)
            dve.wait_ge(hi_done, 1)
            nc.vector.tensor_tensor(w_lo[:, 0, second_half], raw[:, 0, second_half],
                                    w_hi[:, 0, second_half].bitcast(F32), ALU.subtract).then_inc(lo_done, 1)
            for m in range(1, DT):
                x_part(0, m)
            for m in range(1, DT):
                add_squares(0, m)
            ffn_in(U_FFN1_IN, 0, 0)
            ffn_out(U_FFN1_OUT, 0, 1)
            norm(1)

            def bank(a):
                return acc[:, (a + 2) % 4, :]

            def query(dst, u, a):
                dve.wait_ge(unit_done, U_PROJ + u + 1)
                nc.vector.scalar_tensor_tensor(dst, bank(a), HD ** -0.5, R[:], ALU.mult, ALU.mult).then_inc(proj_done, 1)

            def scaled(dst, u, src):
                dve.wait_ge(unit_done, U_PROJ + u + 1)
                nc.vector.tensor_tensor(dst, src, R[:], ALU.mult).then_inc(proj_done, 1)

            def keys_ib(u, a):
                dve.wait_ge(unit_done, U_PROJ + u + 1)
                for dst, half in ((kI, slice(0, HD)), (kB, slice(HD, P))):
                    nc.vector.tensor_tensor(dst[half, :], bank(a)[half, :], R[half, :], ALU.mult).then_inc(proj_done, 1)

            def values_b():
                src = att[:, 3, 0:NB * BVW].rearrange("p (n c) -> p n c", n=NB)
                dve.wait_ge(v_full, 1)
                nc.vector.tensor_scalar(w_idx[:], src[:, :, HD:BVW], HEADS ** -0.5, None, ALU.mult).then_inc(w_idx_done, 1)
                nc.vector.tensor_copy(vB[:], src[:, :, 0:HD]).then_inc(v_done, 1)

            def values_a():
                dve.wait_ge(v_full, 2)
                nc.vector.tensor_copy(vA[:], att[:, 3, :].rearrange("p (n c) -> p n c", n=NB)).then_inc(v_done, 1)

            def add_index(t):
                n, hh = INDEX[t]
                width = (n + 1) * P
                out = score[:, score_at[n]:score_at[n] + width]
                if t == 0:
                    dve.wait_ge(w_idx_done, 1)
                    dve.wait_ge(masks_done, 6)
                dve.wait_ge(relu_done, t + 1)
                if hh:
                    dve.wait_ge(idx_added, t)
                nc.vector.scalar_tensor_tensor(out, probs[:, t % 2, 0:width], w_idx[:, n, hh:hh + 1],
                                               out if hh else causal[:, T - width:T], ALU.mult, ALU.add).then_inc(idx_added, 1)

            rounds = list(range(len(ROUNDS)))

            def scores_of(n):
                return score[:, score_at[n]:score_at[n] + (n + 1) * P]

            def find8(r):
                n, k = ROUNDS[r]
                if k:
                    dve.wait_ge(took8, r - 2)
                elif r == 0:
                    dve.wait_ge(idx_added, len(INDEX))
                nc.vector.max(top8[:, r % 3, :], scores_of(n)).then_inc(top8_done, 1)

            def select(count):
                for r in [rounds.pop(0) for _ in range(min(count, len(rounds)))]:
                    n, k = ROUNDS[r]
                    if r == 0:
                        find8(0)
                    if r + 1 < len(ROUNDS):
                        find8(r + 1)
                    dve.wait_ge(top8_done, r + 1)
                    nc.vector.match_replace(scores_of(n), top8[:, r % 3, :], scores_of(n), TAKEN).then_inc(took8, 1)
                    if k == TOPK // 8 - 1:
                        dve.wait_ge(took8, r + 1)
                        nc.vector.tensor_scalar(scores_of(n), scores_of(n), TAKEN, NEG, ALU.is_gt,
                                                ALU.mult).then_inc(mask_done, 1)

            for u in range(N_PROJ):
                if u == IBK:
                    keys_ib(u, u)
                elif u == BVIW:
                    dve.wait_ge(unit_done, U_PROJ + u + 1)
                    nc.vector.tensor_tensor(bvT[0:BVW, :], bank(u)[0:BVW, :], R[0:BVW, :], ALU.mult).then_inc(proj_done, 1)
                elif u == AV:
                    scaled(avT, u, bank(u))
                elif u == AK:
                    scaled(kA[:], u, bank(u))
                else:
                    q, first = (qI, IQ) if u < BQ else (qB, BQ) if u < AV else (qA, AQ)
                    query(q[:, u - first, :], u, u)
                if u == IQ + 1:
                    values_b()
                if BQ - 1 <= u < BQ + 2:
                    for t in range(HEADS * (u - BQ + 1), HEADS * (u - BQ + 2)):
                        add_index(t)
                elif u == BQ + 2:
                    for hh in range(HEADS):
                        nc.vector.scalar_tensor_tensor(biasA[:, 2 * (hh % 4) + hh // 4, :], dist[:, 2 * P:T], -SLOPES[hh],
                                                       window[:], ALU.mult, ALU.add).then_inc(biasA_done, 1)
                elif BQ + 2 < u < AK:
                    select(ROUNDS_IN_UNIT)
                if u == AQ + 1:
                    values_a()

            def col(s):
                return slice(s % RING, s % RING + 1)

            def bias_b(s):
                kind, n, i, g = STEPS[s]
                width = keys_of(kind, n)[1] * P
                mask = scores_of(n) if n else causal[:, T - P:T]
                b = s - NS // 2
                if b == 0:
                    dve.wait_ge(mask_done, NB - 1)
                if b >= 2:
                    dve.wait_ge(logits_done, s - 1)
                nc.vector.scalar_tensor_tensor(biasB[:, s % 2, 0:width], dist[:, T - width:T], -SLOPES[HEADS + i + 4 * g],
                                               mask, ALU.mult, ALU.add).then_inc(biasB_done, 1)

            def logits(s):
                kind, n, i, g = STEPS[s]
                width = keys_of(kind, n)[1] * P
                w = slice(0, width)
                if kind == "A":
                    bias = biasA[:, 2 * i + g, 2 * P - width:2 * P]
                    if s == 0:
                        dve.wait_ge(biasA_done, HEADS)
                else:
                    bias = biasB[:, s % 2, w]
                    dve.wait_ge(biasB_done, s - NS // 2 + 1)
                dve.wait_ge(s_full, s + 1)
                if s >= RING:
                    dve.wait_ge(pt_full, s - RING + 1)
                nc.vector.tensor_tensor_reduce(out=probs[:, s % RING, w], in0=s_bank(s)[:, w], in1=bias, scale=1.0,
                                               scalar=-3.4e38, op0=ALU.add, op1=ALU.max,
                                               accum_out=row_max[:, col(s)]).then_inc(logits_done, 1)

            def negate_max(s):
                kind, n, i, g = STEPS[s]
                head = i + 4 * g
                dve.wait_ge(logits_done, s + 1)
                if kind == "A":
                    nc.vector.tensor_scalar(neg_max[:, col(s)], row_max[:, col(s)], sink[:, head:head + 1], -1.0,
                                            ALU.max, ALU.mult).then_inc(neg_max_done, 1)
                else:
                    nc.vector.tensor_scalar(neg_max[:, col(s)], row_max[:, col(s)], -1.0, None,
                                            ALU.mult).then_inc(neg_max_done, 1)

            def add_sink(s):
                dve.wait_ge(exp_done, s + 1)
                dve.wait_ge(sink_exp_done, s + 1)
                nc.vector.tensor_tensor(row_sum[:, col(s)], row_sum[:, col(s)], sink_exp[:, col(s)],
                                        ALU.add).then_inc(sum_done, 1)

            def invert_sum(s):
                if STEPS[s][0] == "A":
                    dve.wait_ge(sum_done, s + 1)
                else:
                    dve.wait_ge(exp_done, s + 1)
                nc.vector.reciprocal(row_rcp[:, col(s)], row_sum[:, col(s)]).then_inc(rcp_done, 1)

            def normalise(s):
                kind, n, i, g = STEPS[s]
                w = slice(0, keys_of(kind, n)[1] * P)
                dve.wait_ge(rcp_done, s + 1)
                nc.vector.tensor_scalar(probs[:, s % RING, w], probs[:, s % RING, w], row_rcp[:, col(s)], None,
                                        ALU.mult).then_inc(probs_done, 1)

            def y_lo(pair):
                dst, hi_ = (yA_lo, yA_hi) if pair < PAIRS else (yB_lo, yB_hi)
                i = pair % PAIRS
                dve.wait_ge(y_hi_done, pair + 1)
                nc.vector.tensor_tensor(dst[:, i, :], y_bank(pair), hi_[:, i, :].bitcast(F32), ALU.subtract).then_inc(y_lo_done, 1)

            dve.wait_ge(sink_in, 16)
            for s in range(NS + LAG_PV + LAG_Y + 1):
                last_a, last_b = 1 <= s <= NS // 2, NS // 2 < s <= NS
                if s < NS:
                    logits(s)
                if last_a:
                    add_sink(s - 1)
                if last_b:
                    invert_sum(s - 1)
                if s < NS:
                    negate_max(s)
                if last_a:
                    invert_sum(s - 1)
                if last_b:
                    normalise(s - 1)
                if NS // 2 <= s + 1 < NS:
                    if s + 1 == NS // 2:
                        select(len(rounds))
                    bias_b(s + 1)
                if SELECT_FROM <= s < NS // 2 - 1:
                    select(1)
                if s - LAG_PV >= PER_PAIR and (s - LAG_PV - LAG_Y) % PER_PAIR == 0:
                    y_lo((s - LAG_PV - LAG_Y) // PER_PAIR - 1)
                if s > 4 and s % 4 == 1:
                    gt = s // 4 - 1
                    if gt < N_GATES:
                        scaled(gates[:, gt, :], N_PROJ + gt, gate_bank(gt))

            for m in range(DT):
                pair = (2 * m + 2) % 4
                dve.wait_ge(unit_done, U_BRANCH + m + 1)
                dve.wait_ge(gate_sig, 2 * m + 2)
                if m:
                    dve.wait_ge(mix_lo_done, m)
                nc.vector.tensor_tensor(br[:, 0, :], acc[:, pair, :], gates[:, m, :], ALU.mult).then_inc(br_a, 1)
                nc.vector.tensor_tensor(br[:, 1, :], acc[:, pair + 1, :], gates[:, DT + m, :], ALU.mult).then_inc(br_b, 1)
                dve.wait_ge(br_b, m + 1)
                nc.vector.tensor_tensor(br[:, 0, :], br[:, 0, :], br[:, 1, :], ALU.add).then_inc(mix_done, 1)
                dve.wait_ge(mix_hi_done, m + 1)
                nc.vector.tensor_tensor(mix_lo[:, m, :], br[:, 0, :], mix_hi[:, m, :].bitcast(F32),
                                        ALU.subtract).then_inc(mix_lo_done, 1)
            for m in range(DT):
                dve.wait_ge(unit_done, U_MIXOUT + m + 1)
                nc.vector.tensor_tensor(h[:, m, :], acc[:, (m + 2) % 4, :], h[:, m, :], ALU.add).then_inc(h_done, 1)
                prepare(2, m)
            ffn_in(U_FFN2_IN, FT, 2)
            ffn_out(U_FFN2_OUT, 2 * DT, 3)

            for j in range(PLE_T):
                dve.wait_ge(p_hi_done, j + 1)
                nc.vector.tensor_tensor(p_lo[:, j, :], p_raw[:, j, :], p_hi[:, j, :].bitcast(F32),
                                        ALU.subtract).then_inc(p_lo_done, 1)
            norm(3)
            def gate_value(m, w):
                dve.wait_ge(pg_full, m + 1)
                nc.vector.tensor_tensor(pg_val[:, m % 2, w], acc[:, (2 * m) % 4, w], R[:, w], ALU.mult).then_inc(pg_val_done, 1)

            def gated(m, number, w):
                dve.wait_ge(unit_done, U_PLE + m + 1)
                dve.wait_ge(pg_sig_done, number + 1)
                nc.vector.tensor_tensor(pg_val[:, m % 2, w], acc[:, (2 * m) % 4 + 1, w], pg_sig[:, m % 2, w],
                                        ALU.mult).then_inc(pg_mul, 1)

            def add_gated(m, number, w):
                dve.wait_ge(pg_mul, number + 1)
                nc.vector.tensor_tensor(h[:, m, w], h[:, m, w], pg_val[:, m % 2, w], ALU.add).then_inc(h_done, 1)

            for m in range(DT - 1):
                gate_value(m, slice(0, T))
                gated(m, m, slice(0, T))
                add_gated(m, m, slice(0, T))
                add_squares(4, m)
            for w in HALVES:
                gate_value(DT - 1, w)
            for part, w in enumerate(HALVES):
                gated(DT - 1, DT - 1 + part, w)
            for part, w in enumerate(HALVES):
                add_gated(DT - 1, DT - 1 + part, w)

            dve.wait_ge(stat_first_done, 1)
            nc.vector.tensor_copy(sum_last[:], stat_bank).then_inc(sum_first_done, 1)
            dve.wait_ge(sum_first_done, 1)
            dve.wait_ge(stat_done, 5)
            nc.vector.tensor_tensor(sum_last[:], sum_last[:], stat_bank_last, ALU.add).then_inc(sum_last_done, 1)
            dve.wait_ge(std_done, 5)
            nc.vector.reciprocal(rstd[:], std[:]).then_inc(rstd_done, 1)
            dve.wait_ge(rstd_done, 5)
            nc.vector.tensor_copy(rstd_wide[:], rstd[:].unsqueeze(2).broadcast_to([P, NB, P])).then_inc(wide_done, 1)
            dve.wait_ge(r_full, 5)
            for m in range(DT):
                nc.vector.scalar_tensor_tensor(result[:, m, :], h[:, m, :], gain(4, m), r_bank,
                                               ALU.mult, ALU.mult).then_inc(result_done, 1)

        @block.tensor
        def _(pe):
            mm = nc.tensor.matmul

            def wait_unit(i, c):
                pe.wait_ge(lo_done, 4 * i + (c + 1))

            def product(out, c, b, m_hi, m_lo, start, stop):
                w = slice(b * P, b * P + P)
                mm(out, w_hi[:, c % SPLIT, w], m_hi, start=start, stop=False)
                mm(out, w_hi[:, c % SPLIT, w], m_lo, start=False, stop=False)
                return mm(out, w_lo[:, c % SPLIT, w], m_hi, start=False, stop=stop)

            def x_unit(i, c, out, x0=None, midway=None):
                halves = isinstance(i, int) and c < U_FFN1_IN + 2
                if halves:
                    pe.wait_ge(half_lo_done[c], 1)
                else:
                    wait_unit(i, c)
                for b in range(DT):
                    if midway and b == DT // 2:
                        midway()
                    if halves and b == DT // 2:
                        wait_unit(i, c)
                    if x0 is not None:
                        pe.wait_ge(x_lo_done, x0 + b + 1)
                    last = product(out, c, b, x_hi[:, b, :], x_lo[:, b, :], b == 0, b == DT - 1)
                last.then_inc(unit_done, 1)

            def stats(k):
                pe.wait_ge(sumsq_done, 7 * (k + 1))
                for n in range(NB):
                    last = mm(stat_bank[:, n:n + 1], sumsq[:, n * P:(n + 1) * P], ones[:, 0:1], start=True, stop=True)
                last.then_inc(stat_done, 1)

            def spread(k):
                pe.wait_ge(wide_done, k + 1)
                for n in range(NB):
                    last = nc.tensor.transpose(r_bank[:, n * P:(n + 1) * P], rstd_wide[:, n, :], ident[:])
                last.then_inc(r_full, 1)

            def ffn_in(u0, t0, k):
                for r in range(4):
                    if t0 and r == 0:
                        pe.wait_ge(h_done, 2 * DT - 2)
                    if t0 and r == 2:
                        pe.wait_ge(h_done, 2 * DT)
                    midway = {1: lambda: spread(k)} if k else {2: lambda: stats(k), 3: lambda: spread(k)}
                    x_unit(0, u0 + r, acc[:, (r + k) % 4, :], DT * k if r == 0 else None, midway.get(r))
                    if r == 0 and k:
                        stats(k)
                with pe.Fori(1, FT // 2) as i:
                    for r in range(4):
                        if r % 2 == 0:
                            pe.wait_ge(b_done, 2 * i + (t0 + r // 2 - 1))
                        x_unit(i, u0 + r, acc[:, (r + k) % 4, :])

            def ffn_out(u0, t0, h0):
                def pair_of_tiles(i, c):
                    first = isinstance(i, int) and c == u0
                    for r in range(2):
                        out = acc[:, r + (2 if t0 else 0), :]
                        if first:
                            pe.wait_ge(b_done, t0 + FT - 1)
                        else:
                            m = 2 * i + (c - u0) // 2 + r
                            pe.wait_ge(h_done, m + (h0 - 1))
                        for half in range(2):
                            u = c + 2 * r + half
                            wait_unit(i, u)
                            for b in range(K_OUT):
                                j = half * K_OUT + b
                                if first and r == 0:
                                    pe.wait_ge(g_lo_done, t0 + j + 1)
                                last = product(out, u, b, g_hi[:, j, :], g_lo[:, j, :], j == 0, j == FT - 1)
                            last.then_inc(unit_done, 1)

                pair_of_tiles(0, u0)
                with pe.Fori(1, DT // 2) as i:
                    pair_of_tiles(i, u0)

            def keep_warm(count):
                for _ in range(count):
                    mm(att[:, 0, 0:P], ident[:], ident[:], start=True, stop=True)

            pe.wait_ge(consts_done, 4)
            keep_warm(WARM_UP)
            ffn_in(U_FFN1_IN, 0, 0)
            ffn_out(U_FFN1_OUT, 0, 0)

            def bank(a):
                return acc[:, (a + 2) % 4, :]

            def bank_free(a):
                if a in (2, 3):
                    pe.wait_ge(h_done, DT - 3 + a)
                elif a >= 4:
                    pe.wait_ge(proj_done, a - 2)

            def transpose_values(vT, width):
                for n in range(NB):
                    last = nc.tensor.transpose(att[:, 3, n * width:(n + 1) * width], vT[0:width, n * P:(n + 1) * P],
                                               ident[0:width, 0:width])
                last.then_inc(v_full, 1)

            def index_products(n):
                for hh in range(HEADS):
                    t = INDEX.index((n, hh))
                    half = slice(HD * (hh // 4), HD * (hh // 4) + HD)
                    if t == 0:
                        pe.wait_ge(proj_done, IQ + PAIRS + 1)
                        pe.wait_ge(k_copied, 32)
                    if t == 3:
                        pe.wait_ge(v_done, 1)
                    if t >= 4:
                        pe.wait_ge(relu_done, t - 3)
                    mm(att[:, t % 4, 0:(n + 1) * P], qI[half, hh % 4, n * P:(n + 1) * P], kI[half, 0:(n + 1) * P],
                       start=True, stop=True).then_inc(idx_full, 1)

            def values_b():
                pe.wait_ge(proj_done, BVIW + 2)
                transpose_values(bvT, BVW)

            def values_a():
                pe.wait_ge(proj_done, AV + 2)
                pe.wait_ge(relu_done, len(INDEX))
                transpose_values(avT, P)

            midway = {BVIW: lambda: spread(1), IQ + 1: values_b, BQ: lambda: index_products(3),
                      BQ + 1: lambda: index_products(2), BQ + 2: lambda: index_products(1), AQ + 1: values_a}
            for u in range(N_PROJ):
                bank_free(u)
                x_unit(0, U_PROJ + u, bank(u), DT if u == 0 else None, midway.get(u))
                if u == 0:
                    stats(1)

            def scores(s):
                kind, n, i, g = STEPS[s]
                first, count = keys_of(kind, n)
                half = slice(HD * g, HD * g + HD)
                q, k_ = (qA, kA) if kind == "A" else (qB, kB)
                if s == 0:
                    pe.wait_ge(proj_done, N_PROJ + 1)
                    pe.wait_ge(v_done, 2)
                if s >= 3:
                    pe.wait_ge(logits_done, s - 2)
                mm(s_bank(s)[:, 0:count * P], q[half, i, n * P:(n + 1) * P], k_[half, first * P:(first + count) * P],
                   start=True, stop=True).then_inc(s_full, 1)

            def transposes(s):
                kind, n, i, g = STEPS[s]
                pe.wait_ge(probs_done, s + 1)
                if s >= 1:
                    pe.wait_ge(pt_copied, s)
                for b in range(keys_of(kind, n)[1]):
                    w = slice(b * P, (b + 1) * P)
                    last = nc.tensor.transpose(pt_bank[:, w], probs[:, s % RING, w], ident[:])
                last.then_inc(pt_full, 1)

            def weighted(s):
                kind, n, i, g = STEPS[s]
                first, count = keys_of(kind, n)
                half = slice(HD * g, HD * g + HD)
                pe.wait_ge(pt_copied, s + 1)
                pair = s // PER_PAIR
                if s % PER_PAIR == 0 and pair >= 2:
                    pe.wait_ge(y_lo_done, pair - 1)
                for b in range(count):
                    v = vA[:, first + b, half] if kind == "A" else vB[:, first + b, :]
                    last = mm(y_bank(pair)[half, n * P:(n + 1) * P], v, probsT[:, s % 2, b * P:(b + 1) * P],
                              start=(b == 0), stop=(b == count - 1))
                last.then_inc(pv_done, 1)

            def branch_block(m, b):
                y_h, y_l = (yA_hi, yA_lo) if b < PAIRS else (yB_hi, yB_lo)
                i = b % PAIRS
                if m == 0:
                    pe.wait_ge(y_lo_done, b + 1)
                return product(acc[:, (2 * m + 2) % 4 + b // PAIRS, :], U_BRANCH + m, b, y_h[:, i, :], y_l[:, i, :],
                               i == 0, i == PAIRS - 1)

            for s in range(NS + LAG_PV):
                if 0 < s < NS - 1:
                    scores(s + 1)
                if LAG_T <= s < NS + LAG_T:
                    transposes(s - LAG_T)
                if s < NS:
                    gt, quarter = divmod(s, 4)
                    c = U_GATES + gt
                    if quarter == 0:
                        pe.wait_ge(proj_done, N_PROJ + (gt - 2 if gt < 2 else gt))
                        wait_unit(0, c)
                    for b in (2 * quarter, 2 * quarter + 1):
                        last = product(gate_bank(gt), c, b, x_hi[:, b, :], x_lo[:, b, :], b == 0, b == DT - 1)
                    if quarter == 3:
                        last.then_inc(unit_done, 1)
                if s == 0:
                    scores(0)
                    scores(1)
                if NS <= s < NS + PAIRS:
                    if s == NS:
                        pe.wait_ge(proj_done, N_PROJ + N_GATES)
                        wait_unit(0, U_BRANCH)
                    branch_block(0, s - NS)
                if s >= LAG_PV:
                    weighted(s - LAG_PV)

            for m in range(DT):
                if m < 2:
                    pe.wait_ge(proj_done, N_PROJ + N_GATES + 1)
                else:
                    pe.wait_ge(br_b, m - 1)
                if m:
                    wait_unit(0, U_BRANCH + m)
                for b in range(0 if m else PAIRS, 2 * PAIRS):
                    last = branch_block(m, b)
                last.then_inc(unit_done, 1)
            for m in range(DT):
                c = U_MIXOUT + m
                if m < 4:
                    pe.wait_ge(br_b, DT - 1 + m // 2)
                else:
                    pe.wait_ge(h_done, DT + m - 3)
                wait_unit(0, c)
                for b in range(DT):
                    if m == 0:
                        pe.wait_ge(mix_lo_done, b + 1)
                    last = product(acc[:, (m + 2) % 4, :], c, b, mix_hi[:, b, :], mix_lo[:, b, :], b == 0, b == DT - 1)
                last.then_inc(unit_done, 1)

            ffn_in(U_FFN2_IN, FT, 2)
            ffn_out(U_FFN2_OUT, FT, 2 * DT)

            for m in range(DT):
                b0 = (2 * m) % 4
                c = U_PLE + m
                if m == 1:
                    pe.wait_ge(h_done, 3 * DT)
                if m >= 2:
                    pe.wait_ge(pg_mul, m - 1)
                wait_unit(0, c)
                for b in range(DT):
                    if m == 0:
                        pe.wait_ge(x_lo_done, 3 * DT + b + 1)
                    if m == 1 and b == DT // 2:
                        spread(3)
                    last = product(acc[:, b0, :], c, b, x_hi[:, b, :], x_lo[:, b, :], b == 0, b == DT - 1)
                last.then_inc(pg_full, 1)
                if m == 0:
                    stats(3)
                    pe.wait_ge(p_lo_done, PLE_T)
                for j in range(PLE_T):
                    last = product(acc[:, b0 + 1, :], c, DT + j, p_hi[:, j, :], p_lo[:, j, :], j == 0, j == PLE_T - 1)
                last.then_inc(unit_done, 1)
            pe.wait_ge(sumsq_done, 7 * 4 + DT - 2)
            for n in range(NB):
                last = mm(stat_bank[:, n:n + 1], sumsq[:, n * P:(n + 1) * P], ones[:, 0:1], start=True, stop=True)
            last.then_inc(stat_first_done, 1)
            keep_warm(WARM_GAP)
            for n in range(NB):
                if n % (NB // 2) == 0:
                    pe.wait_ge(sq_done, 5 * DT + n // (NB // 2))
                last = mm(stat_bank_last[:, n:n + 1], squares[:, (DT - 1) % 2, n * P:(n + 1) * P], ones[:, 0:1],
                          start=True, stop=True)
            last.then_inc(stat_done, 1)
            keep_warm(WARM_GAP)
            spread(4)


def _columns(w, cols, width=P):
    k = w.shape[0] // P
    out = np.zeros((len(cols), P, k, P), w.dtype)
    for n, c in enumerate(cols):
        out[n, :, :, 0:len(c)] = w[:, c].reshape(k, P, len(c)).transpose(1, 0, 2)
    return out.reshape(len(cols), P, k * P)


def kernel(**inputs):
    import concourse.bacc as bacc
    from concourse.bass_utils import run_bass_kernel_spmd

    a = {n: np.asarray(v) for n, v in inputs.items()}
    tiles = [np.arange(m * P, (m + 1) * P) for m in range(DT)]

    def feature_major(x):
        return np.ascontiguousarray(x.T.reshape(-1, P, T).transpose(1, 0, 2))

    def ffn_in(w):
        return _columns(w, [np.arange(s * FF + j * P, s * FF + (j + 1) * P) for j in range(FT) for s in range(2)])

    def ffn_out(w):
        u = _columns(w, tiles).reshape(DT, P, 2, K_OUT * P)
        return np.ascontiguousarray(u.transpose(0, 2, 1, 3)).reshape(2 * DT, P, K_OUT * P)

    sizes = dict(aq=512, ak=128, av=128, bq=512, bk=64, bv=64, iq=512, ik=64, iw=8, ga=D, gb=D)
    at, n = {}, 0
    for name, size in sizes.items():
        at[name] = n + np.arange(size)
        n += size
    pair = [np.concatenate([np.arange(i * HD, (i + 1) * HD), np.arange((i + 4) * HD, (i + 5) * HD)])
            for i in range(PAIRS)]
    proj = ([np.concatenate([at["ik"], at["bk"]]), np.concatenate([at["bv"], at["iw"]])]
            + [at["iq"][c] for c in pair] + [at["bq"][c] for c in pair] + [at["av"]]
            + [at["aq"][c] for c in pair] + [at["ak"]])
    gate = [at[s][c] for s in ("ga", "gb") for c in tiles]
    rows = np.concatenate(pair)
    branches = np.concatenate([_columns(a["w_br_a"][0][rows], tiles), _columns(a["w_br_b"][0][rows], tiles)], axis=2)
    mid = np.concatenate([_columns(a["w_in"][0], proj + gate), branches, _columns(a["w_out"][0], tiles)])
    ple = np.concatenate([_columns(a["w_ple_gate"][0], tiles), _columns(a["w_ple_proj"][0], tiles)], axis=2)
    gains = np.stack([a["ln_ffn1"][0], a["ln_mix"][0], a["ln_ffn2"][0], a["ln_ple"][0], a["ln_final"]])

    arrays = {
        "x": feature_major(a["x"][0]),
        "p": feature_major(a["p"][0, 0]),
        "gains": np.ascontiguousarray(gains.reshape(5, DT, P).transpose(2, 0, 1)),
        "sink": np.ascontiguousarray(np.broadcast_to(a["a_sink"][0], (P, HEADS))),
        "w_ffn1_in": ffn_in(a["w_ffn1_in"][0]),
        "w_ffn1_out": ffn_out(a["w_ffn1_out"][0]),
        "w_mid": mid,
        "w_ffn2_in": ffn_in(a["w_ffn2_in"][0]),
        "w_ffn2_out": ffn_out(a["w_ffn2_out"][0]),
        "w_ple": ple,
    }
    nc = bacc.Bacc("TRN2", target_bir_lowering=False, num_devices=1)
    args = [nc.dram_tensor(f"in_{n}", v.shape, mybir.dt.from_np(v.dtype), kind="ExternalInput").ap()
            for n, v in arrays.items()]
    args.append(nc.dram_tensor("out_t", (DT, P, T), F32, kind="ExternalOutput").ap())
    layer(nc, *args)
    r = run_bass_kernel_spmd(nc, [{f"in_{n}": v for n, v in arrays.items()}], core_ids=[0])
    out = r.results[0]["out_t"]
    return np.ascontiguousarray(out.reshape(D, T).T).reshape(1, T, D)
```
